# Optimizing a Trainium2 kernel written in Bass

```python
import jax, jax.numpy as jnp
from jax import lax
import numpy as np

D_MODEL = 1024
BATCH = 1
SEQ = 1024
DEPTH = 1

D_MIX = D_MODEL
NSA_HEADS = 8
NSA_KV_HEADS = 2
NSA_HEAD_DIM = 64
NSA_WIDTH = NSA_HEADS * NSA_HEAD_DIM
NSA_KV_WIDTH = NSA_KV_HEADS * NSA_HEAD_DIM
CMP_LEN = 32
CMP_STRIDE = 16
CMP_HIDDEN = 2 * NSA_HEAD_DIM
SLC_BLOCK = 64
SLC_TOPN = 16
WINDOW = 512
Q_BLOCK = 128
HG_HEADS = 4
HG_KEY_DIM = 128
HG_VAL_DIM = 128
HG_WIDTH = HG_HEADS * HG_VAL_DIM
HG_CHUNK = 64
ROPE_THETA = 500000.0
ROT_DIM = NSA_HEAD_DIM // 4
D_FF = 4 * D_MODEL
EPS = 1e-6
NEG = -1e30
IN_SPLITS = (NSA_WIDTH, NSA_KV_WIDTH, NSA_KV_WIDTH, NSA_KV_WIDTH, NSA_KV_WIDTH,
             NSA_KV_WIDTH, NSA_KV_WIDTH, NSA_HEADS * 3,
             HG_HEADS * HG_KEY_DIM, HG_HEADS * HG_KEY_DIM, HG_WIDTH, HG_WIDTH)
D_IN = sum(IN_SPLITS)

kernel_name = 'hymba_nsa_hgrn2_block'

def rms_norm(x, gain):
    xf = x.astype(jnp.float32)
    y = xf * lax.rsqrt(jnp.mean(xf * xf, axis=-1, keepdims=True) + EPS)
    return (y * gain.astype(jnp.float32)).astype(x.dtype)

def rope(x, cos, sin):
    half = ROT_DIM // 2
    c, s = cos.astype(x.dtype), sin.astype(x.dtype)
    x1, x2 = x[..., :half], x[..., half:ROT_DIM]
    return jnp.concatenate([x1 * c - x2 * s, x2 * c + x1 * s, x[..., ROT_DIM:]], axis=-1)

def masked_softmax(s, mask):
    return jax.nn.softmax(jnp.where(mask, s, NEG), axis=-1) * mask

def cmp_to_slc_matrix(n_cmp, n_slc):
    tok = np.arange(n_cmp)[:, None] * CMP_STRIDE + np.arange(CMP_LEN)[None, :]
    blk = tok // SLC_BLOCK
    return (blk[:, :, None] == np.arange(n_slc)[None, None, :]).mean(axis=1).astype(np.float32)

def nsa_mixer(q, kc, vc, ks, vs, kw, vw, gates, q_gain, k_gain,
              pe_k, w1_k, w2_k, pe_v, w1_v, w2_v, cos, sin):
    B, S, _ = q.shape
    G, HPG, DK = NSA_KV_HEADS, NSA_HEADS // NSA_KV_HEADS, NSA_HEAD_DIM
    dtype = q.dtype
    q = q.reshape(B, S, G, HPG, DK).transpose(0, 2, 3, 1, 4)
    q = rope(rms_norm(q, q_gain), cos, sin)

    def kv_heads(t):
        return t.reshape(B, S, G, DK).transpose(0, 2, 1, 3)

    def prep_k(t):
        return rope(rms_norm(kv_heads(t), k_gain), cos, sin)

    kc, ks, kw = prep_k(kc), prep_k(ks), prep_k(kw)
    vc, vs, vw = kv_heads(vc), kv_heads(vs), kv_heads(vw)
    gates = jax.nn.sigmoid(gates.astype(jnp.float32)).reshape(B, S, G, HPG, 3).transpose(0, 2, 3, 1, 4)

    n_cmp = (S - CMP_LEN) // CMP_STRIDE + 1
    tok_idx = jnp.arange(n_cmp)[:, None] * CMP_STRIDE + jnp.arange(CMP_LEN)[None, :]

    def compress(t, pe, w1, w2):
        blocks = t[:, :, tok_idx] + pe
        flat = blocks.reshape(B, G, n_cmp, CMP_LEN * DK)
        return jax.nn.silu(flat @ w1) @ w2

    kc = compress(kc, pe_k, w1_k, w2_k)
    vc = compress(vc, pe_v, w1_v, w2_v)
    cmp_end = jnp.arange(n_cmp) * CMP_STRIDE + CMP_LEN - 1

    n_slc = S // SLC_BLOCK
    n_top = min(SLC_TOPN, n_slc)
    ks_blocks = ks.reshape(B, G, n_slc, SLC_BLOCK, DK)
    vs_blocks = vs.reshape(B, G, n_slc, SLC_BLOCK, DK)
    slc_map = jnp.asarray(cmp_to_slc_matrix(n_cmp, n_slc))
    kw_pad = jnp.pad(kw, ((0, 0), (0, 0), (WINDOW, 0), (0, 0)))
    vw_pad = jnp.pad(vw, ((0, 0), (0, 0), (WINDOW, 0), (0, 0)))
    scale = DK ** -0.5
    gather = jax.vmap(jax.vmap(lambda blocks, ix: blocks[ix]))
    j_blk = jnp.arange(n_slc)

    def block_fn(blk):
        q0 = blk * Q_BLOCK
        qb = lax.dynamic_slice_in_dim(q, q0, Q_BLOCK, axis=3)
        gb = lax.dynamic_slice_in_dim(gates, q0, Q_BLOCK, axis=3)
        t = q0 + jnp.arange(Q_BLOCK)
        s = jnp.einsum('bghqd,bgnd->bghqn', qb, kc).astype(jnp.float32) * scale
        p_cmp = masked_softmax(s, cmp_end[None, :] <= t[:, None])
        o_cmp = jnp.einsum('bghqn,bgnd->bghqd', p_cmp.astype(dtype), vc)
        imp = jnp.einsum('bghqn,nj->bgqj', p_cmp, slc_map)
        cur = t // SLC_BLOCK
        forced = (j_blk[None, :] == 0) | (j_blk[None, :] == cur[:, None]) | (j_blk[None, :] == cur[:, None] - 1)
        valid = j_blk[None, :] <= cur[:, None]
        imp = jnp.where(forced, jnp.inf, jnp.where(valid, imp, -jnp.inf))
        _, idx = lax.top_k(imp, n_top)
        k_sel = gather(ks_blocks, idx).reshape(B, G, Q_BLOCK, n_top * SLC_BLOCK, DK)
        v_sel = gather(vs_blocks, idx).reshape(B, G, Q_BLOCK, n_top * SLC_BLOCK, DK)
        pos = (idx[..., None] * SLC_BLOCK + jnp.arange(SLC_BLOCK)).reshape(B, G, Q_BLOCK, n_top * SLC_BLOCK)
        s = jnp.einsum('bghqd,bgqkd->bghqk', qb, k_sel).astype(jnp.float32) * scale
        p = masked_softmax(s, (pos <= t[:, None])[:, :, None])
        o_slc = jnp.einsum('bghqk,bgqkd->bghqd', p.astype(dtype), v_sel)
        kwb = lax.dynamic_slice_in_dim(kw_pad, q0, Q_BLOCK + WINDOW, axis=2)
        vwb = lax.dynamic_slice_in_dim(vw_pad, q0, Q_BLOCK + WINDOW, axis=2)
        kpos = q0 - WINDOW + jnp.arange(Q_BLOCK + WINDOW)
        wmask = (kpos[None, :] <= t[:, None]) & (kpos[None, :] > t[:, None] - WINDOW) & (kpos[None, :] >= 0)
        s = jnp.einsum('bghqd,bgkd->bghqk', qb, kwb).astype(jnp.float32) * scale
        p = masked_softmax(s, wmask)
        o_win = jnp.einsum('bghqk,bgkd->bghqd', p.astype(dtype), vwb)
        return (gb[..., 0:1] * o_cmp + gb[..., 1:2] * o_slc + gb[..., 2:3] * o_win).astype(dtype)

    out = lax.map(block_fn, jnp.arange(S // Q_BLOCK))
    return out.transpose(1, 0, 4, 2, 3, 5).reshape(B, S, NSA_WIDTH)

def hgrn2_mixer(q, f_logit, i, g, lb, out_gain):
    B, S, _ = q.shape
    H, DK, DV, C = HG_HEADS, HG_KEY_DIM, HG_VAL_DIM, HG_CHUNK
    n_chunk = S // C
    lbf = lb.astype(jnp.float32)
    f = lbf + (1.0 - lbf) * jax.nn.sigmoid(f_logit.astype(jnp.float32))
    logf = jnp.log(f)
    k = 1.0 - f
    qf = jax.nn.silu(q.astype(jnp.float32))
    v = i.astype(jnp.float32)

    def chunks(t, d):
        return t.reshape(B, n_chunk, C, H, d).transpose(1, 0, 3, 2, 4)

    causal = jnp.tril(jnp.ones((C, C), bool))

    def step(state, xs):
        qc, kc, vc, lc = xs
        bc = jnp.cumsum(lc, axis=2)
        diff = jnp.where(causal[:, :, None], bc[:, :, :, None, :] - bc[:, :, None, :, :], -jnp.inf)
        a = jnp.einsum('bhtd,bhsd,bhtsd->bhts', qc, kc, jnp.exp(diff))
        o = jnp.einsum('bhtd,bhdv->bhtv', qc * jnp.exp(bc), state) + jnp.einsum('bhts,bhsv->bhtv', a, vc)
        b_last = bc[:, :, -1:, :]
        state = jnp.exp(b_last[:, :, 0, :])[..., None] * state + jnp.einsum('bhsd,bhsv->bhdv', kc * jnp.exp(b_last - bc), vc)
        return state, o

    s0 = jnp.zeros((B, H, DK, DV), jnp.float32)
    _, o = lax.scan(step, s0, (chunks(qf, DK), chunks(k, DK), chunks(v, DV), chunks(logf, DK)))
    o = o.transpose(1, 0, 3, 2, 4).reshape(B, S, H, DV)
    o = rms_norm(o, out_gain) * jax.nn.silu(g.astype(jnp.float32).reshape(B, S, H, DV))
    return o.reshape(B, S, HG_WIDTH).astype(q.dtype)

def setup_inputs(seed: int = 0) -> dict:
    key = jax.random.key(seed)
    ks = jax.random.split(key, 18)
    f32 = jnp.float32

    def w(k, shape, fan_in):
        return jax.random.normal(k, shape, f32) * fan_in ** -0.5

    def gain(k, shape):
        return 1.0 + 0.02 * jax.random.normal(k, shape, f32)

    L = DEPTH
    return {
        'x': jax.random.normal(ks[0], (BATCH, SEQ, D_MODEL), f32),
        'attn_norm': gain(ks[1], (L, D_MODEL)),
        'w_in': w(ks[2], (L, D_MODEL, D_IN), D_MODEL),
        'q_norm': gain(ks[3], (L, NSA_HEAD_DIM)),
        'k_norm': gain(ks[4], (L, NSA_HEAD_DIM)),
        'cmp_pe_k': 0.02 * jax.random.normal(ks[5], (L, CMP_LEN, NSA_HEAD_DIM), f32),
        'cmp_w1_k': w(ks[6], (L, CMP_LEN * NSA_HEAD_DIM, CMP_HIDDEN), CMP_LEN * NSA_HEAD_DIM),
        'cmp_w2_k': w(ks[7], (L, CMP_HIDDEN, NSA_HEAD_DIM), CMP_HIDDEN),
        'cmp_pe_v': 0.02 * jax.random.normal(ks[8], (L, CMP_LEN, NSA_HEAD_DIM), f32),
        'cmp_w1_v': w(ks[9], (L, CMP_LEN * NSA_HEAD_DIM, CMP_HIDDEN), CMP_LEN * NSA_HEAD_DIM),
        'cmp_w2_v': w(ks[10], (L, CMP_HIDDEN, NSA_HEAD_DIM), CMP_HIDDEN),
        'nsa_out_norm': gain(ks[11], (L, NSA_WIDTH)),
        'hgrn_lb': 0.5 * jax.random.normal(ks[12], (L + 1, HG_HEADS * HG_KEY_DIM), f32),
        'hgrn_out_norm': gain(ks[13], (L, HG_VAL_DIM)),
        'w_out': w(ks[14], (L, D_MIX, D_MODEL), D_MIX),
        'mlp_norm': gain(ks[15], (L, D_MODEL)),
        'w_mlp_in': w(ks[16], (L, D_MODEL, D_FF), D_MODEL),
        'w_mlp_out': w(ks[17], (L, D_FF, D_MODEL), D_FF),
    }

def reference(x, attn_norm, w_in, q_norm, k_norm, cmp_pe_k, cmp_w1_k, cmp_w2_k,
              cmp_pe_v, cmp_w1_v, cmp_w2_v, nsa_out_norm, hgrn_lb, hgrn_out_norm,
              w_out, mlp_norm, w_mlp_in, w_mlp_out):
    B, S, _ = x.shape
    pos = jnp.arange(S, dtype=jnp.float32)
    inv_freq = ROPE_THETA ** (-jnp.arange(0, ROT_DIM, 2, dtype=jnp.float32) / ROT_DIM)
    ang = pos[:, None] * inv_freq[None, :]
    cos, sin = jnp.cos(ang), jnp.sin(ang)
    lb_all = jnp.cumsum(jax.nn.softmax(hgrn_lb.astype(jnp.float32), axis=0), axis=0)
    split_at = [int(v) for v in np.cumsum(IN_SPLITS)[:-1]]
    for l in range(DEPTH):
        h = rms_norm(x, attn_norm[l])
        proj = h @ w_in[l]
        (nq, nkc, nvc, nks, nvs, nkw, nvw, ngate, hq, hf, hi, hg) = jnp.split(proj, split_at, axis=-1)
        y_nsa = nsa_mixer(nq, nkc, nvc, nks, nvs, nkw, nvw, ngate, q_norm[l], k_norm[l],
                          cmp_pe_k[l], cmp_w1_k[l], cmp_w2_k[l], cmp_pe_v[l], cmp_w1_v[l], cmp_w2_v[l],
                          cos, sin)
        y_nsa = rms_norm(y_nsa, nsa_out_norm[l])
        y_hg = hgrn2_mixer(hq, hf, hi, hg, lb_all[l], hgrn_out_norm[l])
        x = x + jnp.concatenate([y_nsa, y_hg], axis=-1) @ w_out[l]
        h = rms_norm(x, mlp_norm[l])
        x = x + jnp.square(jax.nn.relu(h @ w_mlp_in[l])) @ w_mlp_out[l]
    return x


_drawn_inputs = setup_inputs


def setup_inputs(seed=0):
    import zlib

    import numpy as np

    out = dict(_drawn_inputs(seed))
    spreads = {}
    factors = {'attn_norm': 3.052,
     'q_norm': 7.249,
     'k_norm': 8.0,
     'cmp_pe_k': 47.903,
     'nsa_out_norm': 36.96,
     'hgrn_out_norm': 7.829,
     'mlp_norm': 11.148,
     'cmp_pe_v': 8.0}
    for name, (base, spread) in spreads.items():
        noise = np.random.default_rng([zlib.crc32(name.encode()), seed]).standard_normal(out[name].shape)
        drawn = base * np.exp(spread * noise) if base else spread * noise
        out[name] = __import__('jax').numpy.asarray(drawn.astype(out[name].dtype))
    for name, factor in factors.items():
        out[name] = (out[name] * factor).astype(out[name].dtype)
    return out
```

```python
import numpy as np
import concourse.bass as bass
from concourse import mybir

F32 = mybir.dt.float32
F32R = mybir.dt.float32r
BF16 = mybir.dt.bfloat16
I32 = mybir.dt.int32
ALU = mybir.AluOpType
ACT = mybir.ActivationFunctionType
AX = mybir.AxisListType.X

P = 128
S = 1024
D = 1024
NT = S // P
KC = D // P
NH, NG, DK = 8, 2, 64
HPG = NH // NG
CMP_LEN, CMP_STRIDE = 32, 16
NCMP = (S - CMP_LEN) // CMP_STRIDE + 1
NCP = NCMP + 1
WIN_T = 512 // P
HH = 4
FF = 4096
BW = 512
EPS = 1e-6
NEG = -1e30
Q0, KC0, VC0, KS0, VS0, KW0, VW0, GT0 = 0, 512, 640, 768, 896, 1024, 1152, 1280
NSAW = 1304
HQ0, HI0 = NSAW, NSAW + 1024
NHEADCOL = KW0 // DK + NG
TAIL = NSAW - 2 * BW
LEVELS = [64, 32, 16, 8, 4, 2, 1]
NF = FF // BW


def as_bf16(a):
    return np.ascontiguousarray((a.view(np.uint32) >> 16).astype(np.uint16))


def constants():
    pos = np.arange(S, dtype=np.float32)
    inv = (np.float32(500000.0) ** (-np.arange(0, 16, 2, dtype=np.float32) / np.float32(16))).astype(np.float32)
    ang = (pos[:, None] * inv[None, :]).astype(np.float32)
    rope = np.concatenate([np.cos(ang), np.sin(ang)], axis=1).astype(np.float32)
    i = np.arange(P)
    eye = np.eye(P, dtype=np.float32)
    masks = np.zeros((P, 3 * P), np.float32)
    masks[:, 0:P] = eye
    masks[:, P:2 * P] = np.where(i[None, :] <= i[:, None], 0.0, NEG)
    masks[:, 2 * P:] = np.where(i[None, :] > i[:, None], 0.0, NEG)
    t = (np.arange(NT)[:, None] * P + i[None, :])
    end = np.arange(NCP) * CMP_STRIDE + CMP_LEN - 1
    ok = (end[None, None, :] <= t[:, :, None]) & (np.arange(NCP) < NCMP)[None, None, :]
    cmask = np.where(ok, 0.0, NEG).transpose(1, 0, 2).reshape(P, NT * NCP).astype(np.float32)
    valid = (t >= CMP_LEN - 1).T.astype(np.float32)
    tree = np.zeros((P, (len(LEVELS) + 1) * P), np.int32)
    for n, b in enumerate(LEVELS):
        same = (i[:, None] // (2 * b)) == (i[None, :] // (2 * b))
        tree[:, n * P:(n + 1) * P] = same & (i[:, None] % (2 * b) < b) & (i[None, :] % (2 * b) >= b)
    tree[:, len(LEVELS) * P:] = np.eye(P)
    return {"c_rope": rope, "c_eye": eye, "c_masks": as_bf16(masks), "c_cmask": as_bf16(cmask),
            "c_valid": np.ascontiguousarray(valid), "c_tree": tree}


class Steps:

    def __init__(self, sem):
        self.sem, self.base, self.n = sem, 0, 0

    def mark(self, ins):
        self.n += 1
        return ins.then_inc(self.sem, 1)

    def now(self):
        return self.base + self.n

    def wait(self, eng):
        eng.wait_ge(self.sem, self.now())

    def enter(self, trip, per):
        self.start, self.per = self.base + self.n, per
        self.base, self.n = trip * per + self.start, 0

    def leave(self, trips):
        assert self.n == self.per, (self.n, self.per)
        self.base, self.n = self.start + trips * self.per, 0


class Items:

    def __init__(self):
        self.items = []
        for hh in range(2):
            self.items.append(("cmp", hh, 0, []))
            for t in range(NT):
                self.items.append(("slc", hh, t, list(range(t + 1))))
                self.items.append(("win", hh, t, list(range(max(0, t - WIN_T), t + 1))))
        self.per_head = len(self.items) // 2
        self.groups, self.of = [], {}
        self.prep = {}
        self.order = []
        out = {}
        for j in range(-1, len(self.items)):
            if j == -1:
                self._prep(0)
            elif j == PREP_AT:
                self._prep(1)
            if j >= 0:
                kind, hh, t, tiles = self.items[j]
                n = 4 if kind == "cmp" else len(tiles)
                self.of[j] = []
                for g0 in range(0, n, 4):
                    self.of[j].append(len(self.groups))
                    self.groups.append(dict(item=j, first=g0, n=min(4, n - g0)))
        use_a = use_v = use_pt = 0
        for m, g in enumerate(self.groups):
            if g["item"] is None:
                g["act"], g["dve"] = True, True
            else:
                g["act"] = m % 2 == 0 or g["n"] <= 1
                g["dve"] = not g["act"]
                g["pt"] = use_pt % PT_SLOTS
                g["ptn"] = use_pt
                use_pt += 1
            use_a += g["act"]
            use_v += g["dve"]
            g["act_after"], g["dve_after"] = use_a, use_v
        self.n_act, self.n_dve, self.n_pt = use_a, use_v, use_pt
        assert use_pt % PT_SLOTS == 0 and len(self.groups) % 2 == 0

    def alloc(self, j):
        kind, hh, t, _ = self.items[j]
        return 9 * hh + (0 if kind == "cmp" else 1 + t)

    def _prep(self, hh):
        self.prep[hh] = [len(self.groups), len(self.groups) + 1]
        for half in range(2):
            self.groups.append(dict(item=None, hh=hh, half=half, n=4))


PREP_AT = 9
PT_SLOTS = 5


def program(nc, x, attn_norm, w_in, q_norm, k_norm, cmp_pe_k, cmp_w1_k, cmp_w2_k, cmp_pe_v, cmp_w1_v,
            cmp_w2_v, nsa_out_norm, hgrn_lb, hgrn_out_norm, w_out, mlp_norm, w_mlp_in, w_mlp_out,
            c_rope, c_eye, c_masks, c_cmask, c_valid, c_tree, out):
    at = {"small": 197376}
    base = (nc.sbuf_base + 31) // 32 * 32

    def sb(name, shape, dt, offset=None):
        if offset is None:
            n = 2 if dt == BF16 else 4
            for k in shape[1:]:
                n *= k
            n = (n + 31) // 32 * 32
            offset = at["small"]
            at["small"] += n
        return nc.alloc_sbuf_tensor_at(name, list(shape), dt, offset=base + offset)

    HT_H = sb("hT_high", [P, KC, S], F32R, 0)
    HT_L = sb("hT_low", [P, KC, S], F32R, 32768)
    RING = 4
    w_raw = sb("w_raw", [P, RING, BW], F32, 65536)
    w_high = sb("w_high", [P, RING, BW], F32R, 73728)
    w_low = sb("w_low", [P, RING, BW], F32R, 81920)
    NSA_AT, FM_AT, HV_AT = 90112, 131840, 164608
    nsa = sb("nsa", [P, NT, NSAW], F32, NSA_AT)
    fm = sb("hgrn_qf", [P, 2, NT, HH, P], F32, FM_AT)
    hv = sb("hgrn_vg", [P, 2, NT, HH * P], F32, HV_AT)
    x_in = sb("x_in", [P, NT, D], F32, NSA_AT)
    row = sb("normed_rows", [P, 2, D], F32, FM_AT)
    gain_row = sb("attn_gain", [P, D], F32, FM_AT + 8192)
    junk = sb("squares", [P, 2, D], F32, FM_AT + 12288)
    sq = sb("head_squares", [P, 2, NHEADCOL * DK], F32, HV_AT)
    rtmp = sb("rope_products", [P, 4, 14 * 8], F32, HV_AT + 9216)
    hsum, hrs_a, hrs_t, hrstd = (sb(n, [P, NT, 20], F32, HV_AT + 11264 + 640 * i)
                                 for i, n in enumerate(("h_sums", "h_rsqrt_a", "h_rsqrt_t", "h_rstd")))
    w1 = sb("cmp_w1", [P, 2, CMP_LEN, P], F32, HV_AT)
    kcab = sb("cmp_tokens", [P, 2, S], F32)
    KS_H = sb("k_high", [P, 2, NG, S], F32R, 0)
    KS_L = sb("k_low", [P, 2, NG, S], F32R, 16384)
    QT = sb("q_stack", [P, 2, S], F32R, 32768)
    probs = sb("probs", [P, 2, S], F32, 40960)
    pT = sb("probs_T", [P, PT_SLOTS, BW], F32, 49152)
    masks = sb("masks", [P, 3 * P], BF16, 61440)
    cmask = sb("cmask", [P, NT * NCP], BF16, 62464)
    cdiff = sb("cmp_diff", [P, BW], F32, 59392)
    stage = sb("stage", [P, 2, NT, 2, DK], F32, 197376)
    hk = sb("hgrn_k", [P, NT, BW], F32, 0)
    hlf = sb("hgrn_logf", [P, 2, 2 * BW], F32, 16384)
    hK0 = sb("hgrn_k0", [P, BW], F32, 16384)
    hQ = sb("hgrn_qd", [P, 2, BW], F32, 24576)
    hK = sb("hgrn_kd", [P, 2, BW], F32, 28672)
    hD = sb("hgrn_diff", [P, 2, BW], F32, 32768)
    hE = sb("hgrn_exp", [P, 2, BW], F32, 36864)
    tree = sb("tree_masks", [P, len(LEVELS) + 1, P], I32, 40960)
    hA = sb("hgrn_A", [P, BW], F32, 45056)
    hQe = sb("hgrn_qe", [P, BW], F32, 47104)
    hKd = sb("hgrn_kend", [P, BW], F32, 49152)
    hKT = sb("hgrn_kendT", [P, BW], F32, 51200)
    hst = sb("hgrn_state", [P, BW], F32, 53248)
    hDe = sb("hgrn_dend", [P, BW], F32, 55296)
    hEe = sb("hgrn_eend", [P, 2, BW], F32, 57344)
    hone = sb("hgrn_reset", [P, 2 * BW], F32, 61440)
    x1 = sb("x1", [P, NT, D], F32, FM_AT)
    row2 = sb("mixed_rows", [P, 2, D], F32, 197376)
    h1_H = sb("hidden_high", [P, 4, S], F32R, NSA_AT)
    h1_L = sb("hidden_low", [P, 4, S], F32R, NSA_AT + 16384)
    relu = sb("relu", [P, 4, BW], F32, HV_AT)
    relu2 = sb("relu_squared", [P, 4, BW], F32, HV_AT + 8192)
    junk2 = sb("squares2", [P, 2, D], F32, HV_AT + 16384)
    gain2 = sb("mlp_gain", [P, D], F32, HV_AT + 24576)
    rope = sb("rope", [P, NT, 16], F32)
    eye = sb("eye", [P, P], F32)
    qg = sb("q_gain", [P, DK], F32)
    kg = sb("k_gain", [P, DK], F32)
    gates = sb("gates", [P, NT, 24], F32)
    valid = sb("valid", [P, NT], F32)
    ssq, rs_a, rs_t, rstd = (sb(n, [P, 64], F32) for n in ("sums_of_squares", "rsqrt_a", "rsqrt_t", "rstd"))
    eps = sb("eps", [P, 1], F32)
    pe_sb = sb("pe_rows", [CMP_LEN, 2, 2, DK], F32, 197376)
    peT = sb("peT", [P, 2, CMP_LEN], F32)
    lb_rows = sb("lb_rows", [2 * HH, P], F32, 197376 + 1024)
    negmax = sb("negmax", [P, 34], F32, 63488)
    rsums = sb("row_sums", [P, 2, NT, 2], F32, 63648)
    coef = sb("coef", [P, 2, NT, 2], F32, 63776)
    cmx = sb("cmp_max", [P, 3, NT], F32, 63904)
    lb = sb("lb", [P, 6, HH], F32)
    w2 = sb("cmp_w2", [P, 2, 2, DK], F32)
    kc_H = sb("cmp_k_high", [P, NG, NCP], F32R)
    kc_L = sb("cmp_k_low", [P, NG, NCP], F32R)
    vc = sb("cmp_v", [P, 2, NG, DK], F32)
    assert base + at["small"] <= nc.sbuf_usable_end, (base, at["small"], nc.sbuf_usable_end)
    ps = nc.alloc_psum_tensor("ps", [P, 8, BW], F32)
    ps_bf = None

    def sem(name):
        return nc.alloc_semaphore(name)

    x_loaded = [sem(f"x_loaded{t}") for t in range(NT)]
    c_loaded = sem("constants_loaded")
    pool_set = sem("pool_set")
    w_loaded = [sem(f"w_loaded{i}") for i in range(RING)]
    w_highs = sem("w_highs")
    w_split = sem("w_split")
    w_used = sem("w_used")
    sums_ready = sem("sums_ready")
    logs_ready = sem("logs_ready")
    root_ready = sem("root_ready")
    norm_step = sem("norm_step")
    rows_ready = sem("rows_ready")
    rowsT_done = sem("rowsT_done")
    rows_high = sem("rows_high")
    rows_low = sem("rows_low")
    proj_full = sem("proj_full")
    proj_out = sem("proj_out")

    sq_ready = sem("head_squares_ready")
    sq_summed = sem("head_squares_summed")
    gates_exp = sem("gates_exp")
    prep_step = sem("prep_step")
    prep_done = sem("prep_done")
    c2_loaded = sem("cmp_w1_loaded")
    m_loaded = sem("masks_loaded")
    smallT = sem("pe_and_lb_transposed")
    smallT_out = sem("pe_and_lb_out")
    tokT_done = sem("cmp_tokens_transposed")
    tok_pe = sem("cmp_tokens_pe")
    hid_full = sem("cmp_hidden_full")
    hid_exp = sem("cmp_hidden_exp")
    hid_step = sem("cmp_hidden_step")
    hid_ready = sem("cmp_hidden_ready")
    cmp_full = sem("cmp_full")
    cmp_high = sem("cmp_high")
    cmp_low = sem("cmp_low")
    lb_exp = sem("lb_exp")
    pre_exp = sem("pre_exp")
    pre_step = sem("pre_step")
    pre_done = sem("pre_done")

    stage_ready = sem("stage_ready")
    t_full = sem("t_full")
    t_act = sem("t_bank_emptied_by_act")
    t_dve = sem("t_bank_emptied_by_dve")
    qk_done = sem("qk_done")
    max_done = sem("max_done")
    exp_done = sem("exp_done")
    csum_done = sem("csum_done")
    pv_done = sem("pv_done")
    o_free = sem("o_free")
    att_step = sem("att_step")

    t_loaded = sem("tree_masks_loaded")
    fill_set = sem("hgrn_fill")
    ln_done = sem("hgrn_ln")
    k_done = sem("hgrn_one_minus_f")
    bc_done = sem("hgrn_sums")
    d_ready = sem("hgrn_d_ready")
    e_half = sem("hgrn_e_half")
    e_ready = sem("hgrn_e_ready")
    q_ready = sem("hgrn_q_ready")
    kk_ready = sem("hgrn_k_ready")
    k0_ready = sem("hgrn_k0_ready")
    A_full = sem("hgrn_A_full")
    A_merged = sem("hgrn_A_merged")
    eb_ready = sem("hgrn_exp_sums")
    de_ready = sem("hgrn_dend_ready")
    ee_ready = sem("hgrn_exp_end")
    qe_ready = sem("hgrn_qe_ready")
    kd_ready = sem("hgrn_kend_ready")
    KT_full = sem("hgrn_kendT_full")
    KT_ready = sem("hgrn_kendT_ready")
    st_full = sem("hgrn_outputs_full")
    ho_out = sem("hgrn_output_out")
    st_ready = sem("hgrn_state_ready")
    st_step = sem("hgrn_state_step")
    g_loaded = sem("mix_gains_loaded")
    g2_loaded = sem("mlp_gain_loaded")
    x2_loaded = sem("x_loaded_again")
    ysum_ready = sem("ysum_ready")
    osq_ready = sem("osq_ready")
    eg_ready = sem("eg_ready")
    osq_summed = sem("osq_summed")
    mix_step = sem("mix_step")
    mg_ready = sem("hgrn_gates_ready")
    res_out = sem("residual_out")
    wo_full = sem("w_out_full")
    sum2_ready = sem("sum2_ready")
    m1_full = sem("hidden_full")
    m1_out = sem("hidden_out")
    sqd = sem("hidden_squared")
    h_high = sem("hidden_high_ready")
    h_low = sem("hidden_low_ready")
    m2_full = sem("mlp_out_full")
    out_sent = sem("out_sent")

    waits_passed = [sem("pool_waits_passed"), sem("dve_waits_passed")]

    NCONST = 14

    def stand_alone(eng):
        eng.sem_inc(waits_passed[eng is nc.vector])

    chunk_no = {"sp": 0, "pool": 0, "pe": 0}

    def load_chunk(eng, n, j, src, width=BW, first=False):
        if not first:
            eng.wait_ge(w_split, n + j - RING + 1)
        eng.dma_start(w_raw[:, j % RING, 0:width], src).then_inc(w_loaded[j % RING], 16)

    def split_chunk(eng, n, n4, j, width=BW, first=False):
        s = j % RING
        eng.wait_ge(w_loaded[s], (n4 + j // RING + 1) * 16)
        if not first:
            eng.wait_ge(w_used, n + j - RING + 1)
        stand_alone(eng)
        eng.tensor_copy(w_high[:, s, 0:width], w_raw[:, s, 0:width]).then_inc(w_highs, 1)
        eng.wait_ge(w_highs, n + j + 1)
        eng.tensor_tensor(w_low[:, s, 0:width], w_raw[:, s, 0:width],
                          w_high[:, s, 0:width].bitcast(F32), ALU.subtract).then_inc(w_split, 1)

    def three_passes(out_ap, a_hl, b_hl, first, last):
        ins = None
        for n, (i, j) in enumerate(((0, 0), (0, 1), (1, 0))):
            ins = nc.tensor.matmul(out_ap, a_hl[i], b_hl[j], start=first and n == 0, stop=last and n == 2)
        return ins

    def chunk_signals(ins, b, k, full):
        if b == 7:
            ins.then_inc(w_used, 1)
        elif k == KC - 1:
            ins.then_inc(full, 1)

    def rows_chunk(pe, n, j, width, full, bank_free=None):
        s, k = j % RING, j % KC
        pe.wait_ge(w_split, n + j + 1)
        for t in range(NT):
            if k == 0 and bank_free is not None:
                bank_free(t)
            a = [h[:, k, t * P:(t + 1) * P] for h in (HT_H, HT_L)]
            b = [w[:, s, 0:width] for w in (w_high, w_low)]
            chunk_signals(three_passes(ps[:, t, 0:width], a, b, k == 0, k == KC - 1), t, k, full)

    def cols_chunk(pe, n, j, full, bank_free=None):
        s, k = j % RING, j % KC
        pe.wait_ge(w_split, n + j + 1)
        for b in range(8):
            c, half = divmod(b, 2)
            if k == 0 and bank_free is not None:
                bank_free(b)
            a = [w[:, s, c * P:(c + 1) * P] for w in (w_high, w_low)]
            r = [h[:, k, half * BW:(half + 1) * BW] for h in (HT_H, HT_L)]
            chunk_signals(three_passes(ps[:, b, :], a, r, k == 0, k == KC - 1), b, k, full)

    def transpose_rows(pe, r, t, src):
        pe.wait_ge(rows_ready, NT * r + t + 1)
        for j in range(2):
            n = 2 * t + j
            if n >= 4:
                pe.wait_ge(rows_low, 16 * r + n - 3)
            for q in range(4):
                c = 4 * j + q
                ins = nc.tensor.transpose(ps[:, n % 4, q * P:(q + 1) * P], src[:, t % 2, c * P:(c + 1) * P], eye[:])
            ins.then_inc(rowsT_done, 1)

    def hT_slice(h, j, t):
        return h[:, 4 * j:4 * j + 4, t * P:(t + 1) * P]

    def bank4(b):
        return ps[:, b, :].rearrange("p (q c) -> p q c", q=4)

    def high_rows(act, r, t):
        for j in range(2):
            n = 2 * t + j
            act.wait_ge(rowsT_done, 16 * r + n + 1)
            nc.scalar.activation(hT_slice(HT_H, j, t), bank4(n % 4), ACT.Copy).then_inc(rows_high, 1)

    def low_rows(dve, r, t):
        for j in range(2):
            n = 2 * t + j
            dve.wait_ge(rows_high, 16 * r + n + 1)
            nc.vector.tensor_tensor(hT_slice(HT_L, j, t), bank4(n % 4), hT_slice(HT_H, j, t).bitcast(F32),
                                    ALU.subtract).then_inc(rows_low, 1)

    roots = {"act": 0, "dve": 0}
    vnorm = Steps(norm_step)

    norm_bufs = (ssq, rs_a, rs_t, rstd)

    head_bufs = [b[:, :, 0:NHEADCOL] for b in (hsum, hrs_a, hrs_t, hrstd)]

    def cols_of(a, b):
        return [x[:, a:b] for x in norm_bufs]

    def root_act(act, bufs, width):
        sums, _, log, root = bufs
        n = roots["act"] = roots["act"] + 1
        act.activation(log, sums, ACT.Ln, bias=eps[:, 0:1], scale=1.0 / width).then_inc(logs_ready, 1)
        act.wait_ge(logs_ready, n)
        act.activation(root, log, ACT.Exp, scale=-0.5).then_inc(root_ready, 1)

    def root_dve(dve, bufs, width):
        n = roots["dve"] = roots["dve"] + 1
        dve.wait_ge(root_ready, n)
        sums, a, t, r = bufs
        vnorm.mark(dve.tensor_scalar(a, sums, 1.0 / width, EPS, ALU.mult, ALU.add))
        vnorm.mark(dve.tensor_tensor(t, r, r, ALU.mult))
        vnorm.wait(dve)
        vnorm.mark(dve.tensor_tensor(t, t, a, ALU.mult))
        vnorm.wait(dve)
        vnorm.mark(dve.tensor_scalar(t, t, -0.5, 1.5, ALU.mult, ALU.add))
        vnorm.wait(dve)
        vnorm.mark(dve.tensor_tensor(r, r, t, ALU.mult))
        vnorm.wait(dve)

    hid2 = nsa[:, 0, KC0:KC0 + 2 * P]
    hid_e = nsa[:, 1, KC0:KC0 + P].rearrange("p (g n) -> p g n", g=NG)[:, :, 0:NCMP]
    hid_ps = ps[:, 5:7, 0:NCMP]
    pre_x = [fm[:, n // 4, 2 * (n % 4):2 * (n % 4) + 2, :, :].rearrange("p c h t -> p (c h t)") for n in range(8)]
    pre_e = [kcab[:, i, :] for i in range(2)]

    it = Items()

    def key_stack(tensor, m):
        return tensor[:, m // 4, (m // 2) % 2, (m % 2) * BW:(m % 2 + 1) * BW]

    def stack_half(pe, m, slot, half):
        for q in range(4):
            ins = nc.tensor.transpose(ps[:, 4 + m % 2, q * P:(q + 1) * P],
                                      stage[:, slot, 4 * half + q, :, :].rearrange("p a d -> p (a d)"), eye[:])
        ins.then_inc(t_full, 1)

    def scores_view(j):
        w = len(it.items[j][3]) * P
        b = 2 * (j % 2)
        return ps[:, b, 0:w] if w <= BW else ps[:, b:b + 2, 0:w // 2]

    def pt_free(eng, m, ib):
        n = it.groups[m]["ptn"] - PT_SLOTS
        if n >= 0:
            old = [u for u in it.groups if u.get("ptn") == n][0]
            eng.wait_ge(pv_done, ib + (old["item"] + 1))

    def tree_halves(ap, b):
        v = ap.rearrange("p (n c) -> p n c", c=2 * b)
        return v[:, :, 0:b], v[:, :, b:2 * b]

    def per_head(ap):
        return ap.rearrange("p (h t) -> p h t", h=HH)

    ngain = nsa[:, 0, KC0:KC0 + BW]
    hgain = nsa[:, 0, KW0:KW0 + P]
    eg = [nsa[:, 1 + i, KC0:KC0 + BW] for i in range(2)]
    junk_mix = [nsa[:, 5 + i, KC0:KC0 + BW] for i in range(2)]
    osq = [nsa[:, 3 + i, KC0:KC0 + BW] for i in range(2)]

    w_in0 = w_in[0]
    blocks = [(2 * BW, TAIL), (0, BW), (BW, BW), (HQ0, BW), (HQ0 + BW, BW), (HI0, BW), (HI0 + BW, BW)]
    W_OUT_AT = 8 * len(blocks)
    MLP_AT = W_OUT_AT + 16

    with nc.Block() as block:

        @block.sync
        def _(sp):
            for t in range(NT):
                sp.dma_start(x_in[:, t, :], x[0, t * P:(t + 1) * P, :]).then_inc(x_loaded[t], 16)
            for j in range(KC):
                load_chunk(sp, 0, j, w_in0[j * P:(j + 1) * P, 2 * BW:NSAW], TAIL, first=j < RING)
            for pair, col0 in enumerate((0, HQ0, HI0)):
                if pair == 2:
                    sp.wait_ge(prep_done, 1)
                    for kv, w in enumerate((cmp_w1_k, cmp_w1_v)):
                        for a in range(2):
                            sp.dma_start(w1[a * DK:(a + 1) * DK, kv, :, :], w[0].rearrange("(j d) h -> d j h", d=DK))\
                                .then_inc(c2_loaded, 16)
                with sp.Fori(0, 2) as i:
                    n = (i + (1 + 2 * pair)) * KC
                    for j in range(KC):
                        load_chunk(sp, n, j, w_in0[j * P:(j + 1) * P, bass.ds(i * BW + col0, BW)])
            sp.wait_ge(w_used, 8 * len(blocks))
            sp.dma_start(masks[:], c_masks.bitcast(BF16)).then_inc(m_loaded, 16)
            sp.dma_start(cmask[:], c_cmask.bitcast(BF16)).then_inc(m_loaded, 16)
            for blk in range(2):
                for k in range(KC):
                    if blk == 0 and k == RING:
                        sp.wait_ge(o_free, 72)
                        sp.dma_start(tree[:, :, :].rearrange("p n t -> p (n t)"), c_tree).then_inc(t_loaded, 16)
                        sp.dma_start(ngain, nsa_out_norm[0].partition_broadcast(P)).then_inc(g_loaded, 16)
                        sp.dma_start(hgain, hgrn_out_norm[0].partition_broadcast(P)).then_inc(g_loaded, 16)
                        sp.wait_ge(st_ready, NT + 1)
                        for t in range(NT):
                            sp.dma_start(x1[:, t, :], x[0, t * P:(t + 1) * P, :]).then_inc(x2_loaded, 16)
                    load_chunk(sp, W_OUT_AT, blk * KC + k, w_out[0, k * P:(k + 1) * P, blk * BW:(blk + 1) * BW])
            sp.wait_ge(rows_ready, 2 * NT)
            sp.dma_start(gain2[:], mlp_norm[0].partition_broadcast(P)).then_inc(g2_loaded, 16)
            with sp.Fori(0, NF) as i:
                for j in range(KC):
                    load_chunk(sp, i * 16 + MLP_AT, j, w_mlp_in[0, j * P:(j + 1) * P, bass.ds(i * BW, BW)])
                for j in range(KC):
                    half, fc = divmod(j, 4)
                    load_chunk(sp, i * 16 + MLP_AT, KC + j,
                               w_mlp_out[0, bass.ds(i * BW + fc * P, P), half * BW:(half + 1) * BW])
            for t in range(NT):
                sp.wait_ge(res_out, 16 * (NF + 1) - NT + t + 1)
                sp.dma_start(out[0, t * P:(t + 1) * P, :], x1[:, t, :]).then_inc(out_sent, 16)
            sp.wait_ge(out_sent, 16 * NT)

        @block.gpsimd
        def _(pool):
            pool.memset(eps[:], EPS).then_inc(pool_set, 1)
            pool.memset(vc[:], 0.0).then_inc(pool_set, 1)
            pool.wait_ge(pool_set, 2)
            for j in range(KC):
                split_chunk(pool, 0, 0, j, TAIL, first=j < RING)
            for pair in range(3):
                with pool.Fori(0, 2) as i:
                    for j in range(KC):
                        split_chunk(pool, (i + (1 + 2 * pair)) * KC, (i + (1 + 2 * pair)) * 2, j)

            def stage_head(n, slot, src):
                pool.tensor_copy(stage[:, slot, :, :, :], src.unsqueeze(2).to_broadcast([P, NT, 2, DK])).then_inc(stage_ready, 1)

            pool.wait_ge(pre_done, 8)
            for n in range(4):
                if n >= 2:
                    pool.wait_ge(t_full, 2 * (n - 1))
                col = (KS0, KW0)[n // 2] + (n % 2) * DK
                stage_head(n, n % 2, nsa[:, :, col:col + DK])
            with pool.Fori(0, NG) as g:
                with pool.Fori(0, 2) as pr:
                    for hh in range(2):
                        pool.wait_ge(t_full, (g * 2 + pr) * len(it.groups) + (6 + 2 * hh))
                        stand_alone(pool)
                        stage_head(None, hh, nsa[:, :, bass.ds(g * 256 + pr * 128 + hh * DK, DK)])
            pool.wait_ge(o_free, 72)
            pool.memset(hone[:], 1.0).then_inc(fill_set, 1)
            pool.memset(hA[:], 0.0).then_inc(fill_set, 1)
            pool.memset(hQ[:, :, :], 0.0).then_inc(fill_set, 1)
            pool.memset(hK[:, :, :], 0.0).then_inc(fill_set, 1)
            pool.wait_ge(fill_set, 1)
            pool.memset(hone[:].rearrange("p (n t) -> p n t", t=P)[:, :, 0:1], 0.0).then_inc(fill_set, 1)
            for n in range(4):
                f2 = fm[:, 1, 2 * n:2 * n + 2, :, :].rearrange("p c h t -> p (c h t)")
                pool.tensor_scalar(hk[:, 2 * n:2 * n + 2, :].rearrange("p c x -> p (c x)"), f2, -1.0, 1.0,
                                   ALU.mult, ALU.add).then_inc(k_done, 1)
            pool.wait_ge(bc_done, 4)
            with pool.Fori(0, NT) as c:
                bc = fm[:, 1, bass.ds(c, 1), :, :].rearrange("p a h t -> p (a h t)")
                k_c = hk[:, bass.ds(c, 1), :].rearrange("p a x -> p (a x)")

                def keys(n):
                    pool.wait_ge(e_ready, c * 7 + (n + 1))
                    if n == 0:
                        pool.wait_ge(st_ready, c + 1)
                        stand_alone(pool)
                        pool.tensor_copy(hK0[:], k_c).then_inc(k0_ready, 1)
                    if n >= 2:
                        pool.wait_ge(A_full, c * 8 + (n - 1))
                    stand_alone(pool)
                    pool.tensor_tensor(tree_halves(hK[:, n % 2, :], LEVELS[n])[0], tree_halves(k_c, LEVELS[n])[0],
                                       tree_halves(hE[:, n % 2, :], LEVELS[n])[0], ALU.mult).then_inc(kk_ready, 1)

                for n, b in enumerate(LEVELS):
                    if n >= 2:
                        pool.wait_ge(e_ready, c * 7 + (n - 1))
                        stand_alone(pool)
                    v = bc.rearrange("p (n c) -> p n c", c=2 * b)
                    pool.tensor_tensor(hD[:, n % 2, :].rearrange("p (n c) -> p n c", c=2 * b), v,
                                       v[:, :, b - 1:b].to_broadcast([P, BW // (2 * b), 2 * b]), ALU.subtract)\
                        .then_inc(d_ready, 1)
                    if n:
                        keys(n - 1)
                keys(len(LEVELS) - 1)
                v = per_head(bc)
                pool.tensor_tensor(per_head(hDe[:]), v[:, :, P - 1:P].to_broadcast([P, HH, P]), v, ALU.subtract)\
                    .then_inc(de_ready, 1)
                pool.wait_ge(ee_ready, c + 1)
                stand_alone(pool)
                pool.tensor_tensor(hKd[:], k_c, hEe[:, 1, :], ALU.mult).then_inc(kd_ready, 1)
            for j in range(16):
                split_chunk(pool, W_OUT_AT, W_OUT_AT // RING, j)
            with pool.Fori(0, NF) as i:
                for j in range(16):
                    split_chunk(pool, i * 16 + MLP_AT, i * 4 + MLP_AT // RING, j)

        @block.scalar
        def _(act):
            for dst, src in ((rope[:, :, :], c_rope.rearrange("(t p) c -> p t c", p=P)), (eye[:], c_eye),
                             (valid[:], c_valid),
                             (gain_row[:], attn_norm[0].partition_broadcast(P)),
                             (qg[:], q_norm[0].partition_broadcast(P)), (kg[:], k_norm[0].partition_broadcast(P)),
                             (pe_sb[:, 0, 0, :], cmp_pe_k[0]), (pe_sb[:, 0, 1, :], cmp_pe_k[0]),
                             (pe_sb[:, 1, 0, :], cmp_pe_v[0]), (pe_sb[:, 1, 1, :], cmp_pe_v[0]),
                             (w2[:, 0, 0, :], cmp_w2_k[0]), (w2[:, 0, 1, :], cmp_w2_k[0]),
                             (w2[:, 1, 0, :], cmp_w2_v[0]), (lb_rows[:], hgrn_lb.rearrange("l (h d) -> (l h) d", d=P))):
                act.dma_start(dst, src).then_inc(c_loaded, 16)
            act.wait_ge(pool_set, 1)
            for g in range(2):
                for t in range(4 * g, 4 * g + 4):
                    act.wait_ge(x_loaded[t], 16)
                    act.activation(junk[:, t % 2, :], x_in[:, t, :], ACT.Square, accum_out=ssq[:, t:t + 1])\
                        .then_inc(sums_ready, 1)
                    act.wait_ge(sums_ready, t + 1)
                root_act(act, cols_of(4 * g, 4 * g + 4), D)
                if g:
                    for t in range(4):
                        high_rows(act, 0, t)
            for t in range(4, NT):
                high_rows(act, 0, t)

            def evacuate(b, blk, dst):
                if b < 7:
                    act.wait_ge(proj_full, blk * 7 + b + 1)
                else:
                    act.wait_ge(w_used, (blk + 1) * KC)
                act.activation(dst, ps[:, b, 0:dst.shape[-1]] if len(dst.shape) == 2 else
                               ps[:, b, :].rearrange("p (c t) -> p c t", t=P), ACT.Copy).then_inc(proj_out, 1)

            for t in range(NT):
                evacuate(t, 0, nsa[:, t, 2 * BW:NSAW])
            with act.Fori(0, 2) as i:
                for t in range(NT):
                    evacuate(t, i + 1, nsa[:, t, bass.ds(i * BW, BW)])
            for t in range(NT):
                if t >= 2:
                    act.wait_ge(sq_summed, t - 1)
                else:
                    act.wait_ge(proj_out, 24)
                act.activation(sq[:, t % 2, :], nsa[:, t, 0:NHEADCOL * DK], ACT.Square).then_inc(sq_ready, 1)
            act.activation(gates[:, :, :], nsa[:, :, GT0:NSAW], ACT.Exp, scale=-1.0).then_inc(gates_exp, 1)
            act.wait_ge(sq_summed, NT)
            root_act(act, head_bufs, DK)
            with act.Fori(0, 2) as i:
                for b in range(8):
                    c, half = divmod(b, 2)
                    evacuate(b, i + 3, fm[:, bass.ds(i, 1), 4 * half:4 * half + 4, c, :].rearrange("p a c t -> p (a c) t"))
            act.wait_ge(smallT, 1)
            act.activation(peT[:, :, :].rearrange("p a j -> p (a j)"), ps[:, 0, 0:2 * CMP_LEN], ACT.Copy).then_inc(smallT_out, 1)
            act.activation(lb[:, 0:2, :].rearrange("p a h -> p (a h)"), ps[:, 0, 64:64 + 2 * HH], ACT.Copy).then_inc(smallT_out, 1)
            act.wait_ge(hid_step, 3)
            act.activation(lb[:, 2:4, :], lb[:, 2:4, :], ACT.Exp).then_inc(lb_exp, 1)
            for kv in range(2):
                act.wait_ge(hid_full, kv + 1)
                act.activation(hid_e, hid_ps, ACT.Exp, scale=-1.0).then_inc(hid_exp, 1)
                act.wait_ge(cmp_full, kv + 1)
                if kv == 0:
                    act.activation(kc_H[:, :, :].rearrange("p g n -> p (g n)"), ps[:, 0, 0:P], ACT.Copy).then_inc(cmp_high, 1)
            act.wait_ge(pool_set, 2)
            for a in range(2):
                act.activation(vc[a * DK:(a + 1) * DK, a, :, :].rearrange("p g d -> p (g d)"),
                               ps[a * DK:(a + 1) * DK, 7, 0:P], ACT.Copy).then_inc(cmp_high, 1)
            for n in range(8):
                if n >= 2:
                    act.wait_ge(pre_done, n - 1)
                else:
                    act.wait_ge(proj_out, 40)
                act.activation(pre_e[n % 2], pre_x[n], ACT.Exp, scale=-1.0).then_inc(pre_exp, 1)
            with act.Fori(0, 2) as i:
                for t in range(NT):
                    evacuate(t, i + 5, hv[:, bass.ds(i, 1), t, :].rearrange("p a c -> p (a c)"))

            for m in range(8):
                act.wait_ge(t_full, m + 1)
                act.activation(key_stack(KS_H, m), ps[:, 4 + m % 2, :], ACT.Copy).then_inc(t_act, 1)

            def att_act(g, pr):
                i = g * 2 + pr
                tb, ab, ib = i * len(it.groups) + 8, i * it.n_act + 8, i * len(it.items)

                def prep(hh):
                    for half, m in enumerate(it.prep[hh]):
                        act.wait_ge(t_full, tb + (m + 1))
                        act.activation(QT[:, hh, half * BW:(half + 1) * BW], ps[:, 4 + m % 2, :], ACT.Copy).then_inc(t_act, 1)

                def exponentials(j):
                    kind, hh, t, tiles = it.items[j]
                    act.wait_ge(max_done, ib + (j + 1))
                    act.wait_ge(t_full, tb + (it.of[j - 2][-1] + 1 if j >= 2 else 0))
                    if kind == "cmp":
                        act.activation(probs[:, j % 2, 0:BW], cdiff[:], ACT.Exp).then_inc(exp_done, 1)
                        return
                    if j in (2, it.per_head + 2):
                        act.wait_ge(csum_done, i * 2 + (hh + 1))
                    sv = scores_view(j)
                    w = len(tiles) * P
                    o = probs[:, j % 2, 0:w]
                    if len(sv.shape) == 3:
                        o = o.rearrange("p (a b) -> p a b", a=2)
                    act.activation(o, sv, ACT.Exp, bias=negmax[:, j:j + 1],
                                   accum_out=rsums[:, hh, t, int(kind == "win"):int(kind == "win") + 1]).then_inc(exp_done, 1)

                prep(0)
                exponentials(0)
                for j in range(len(it.items)):
                    if j == PREP_AT:
                        prep(1)
                    for m in it.of[j]:
                        if it.groups[m]["act"]:
                            act.wait_ge(t_full, tb + (m + 1))
                            pt_free(act, m, ib)
                            n = it.groups[m]["n"] * P
                            act.activation(pT[:, it.groups[m]["pt"], 0:n], ps[:, 4 + m % 2, 0:n], ACT.Copy).then_inc(t_act, 1)
                    if j + 1 < len(it.items):
                        exponentials(j + 1)

            with act.Fori(0, NG) as g:
                with act.Fori(0, 2) as pr:
                    att_act(g, pr)

            act.wait_ge(o_free, 72)
            for n in range(4):
                f2 = fm[:, 1, 2 * n:2 * n + 2, :, :].rearrange("p c h t -> p (c h t)")
                if n >= 2:
                    act.wait_ge(bc_done, n - 1)
                act.activation(hlf[:, n % 2, :], f2, ACT.Ln).then_inc(ln_done, 1)
            with act.Fori(0, NT) as c:
                bc = fm[:, 1, bass.ds(c, 1), :, :].rearrange("p a h t -> p (a h t)")
                for n, b in enumerate(LEVELS):
                    act.wait_ge(d_ready, c * 7 + (n + 1))
                    if n >= 2:
                        act.wait_ge(q_ready, c * 7 + (n - 1))
                        act.wait_ge(kk_ready, c * 7 + (n - 1))
                    (d1, d2), (e1, e2) = tree_halves(hD[:, n % 2, :], b), tree_halves(hE[:, n % 2, :], b)
                    act.activation(e2, d2, ACT.Exp).then_inc(e_half, 1)
                    act.activation(e1, d1, ACT.Exp, scale=-1.0).then_inc(e_ready, 1)
                act.wait_ge(st_ready, c + 1)
                act.activation(hEe[:, 0, :], bc, ACT.Exp).then_inc(eb_ready, 1)
                act.wait_ge(de_ready, c + 1)
                act.activation(hEe[:, 1, :], hDe[:], ACT.Exp).then_inc(ee_ready, 1)
                act.wait_ge(KT_full, c + 1)
                act.activation(hKT[:], ps[:, 3, :], ACT.Copy).then_inc(KT_ready, 1)
                act.wait_ge(st_full, c + 1)
                act.activation(hv[:, 0, bass.ds(c, 1), :].rearrange("p a x -> p (a x)"), ps[:, 2, :], ACT.Copy)\
                    .then_inc(ho_out, 1)

            act.wait_ge(st_ready, NT + 1)
            act.wait_ge(ho_out, NT)
            for t in range(NT):
                if t >= 2:
                    act.wait_ge(ysum_ready, t - 1)
                act.activation(junk_mix[t % 2], nsa[:, t, 0:BW], ACT.Square, accum_out=ssq[:, t:t + 1]).then_inc(ysum_ready, 1)
                if t >= 2:
                    act.wait_ge(osq_summed, t - 1)
                act.activation(osq[t % 2], hv[:, 0, t, :], ACT.Square).then_inc(osq_ready, 1)
                if t >= 2:
                    act.wait_ge(mg_ready, t - 1)
                act.activation(eg[t % 2], hv[:, 1, t, :], ACT.Exp, scale=-1.0).then_inc(eg_ready, 1)
            act.wait_ge(ysum_ready, NT)
            root_act(act, cols_of(0, NT), BW)
            act.wait_ge(osq_summed, NT)
            root_act(act, cols_of(NT, NT + NT * HH), P)
            for t in range(NT):
                high_rows(act, 1, t)

            for g in range(2):
                for t in range(4 * g, 4 * g + 4):
                    act.wait_ge(res_out, NT + t + 1)
                    if t >= 2:
                        act.wait_ge(sum2_ready, t - 1)
                    act.activation(junk2[:, t % 2, :], x1[:, t, :], ACT.Square, accum_out=ssq[:, 48 + t:49 + t]).then_inc(sum2_ready, 1)
                act.wait_ge(sum2_ready, 4 * (g + 1))
                root_act(act, cols_of(48 + 4 * g, 52 + 4 * g), D)
            for t in range(NT):
                high_rows(act, 2, t)

            with act.Fori(0, NF) as i:
                def high(b):
                    act.wait_ge(sqd, i * 8 + (b + 1))
                    c, half = divmod(b, 2)
                    act.activation(h1_H[:, c, half * BW:(half + 1) * BW], relu2[:, b % 4, :], ACT.Copy).then_inc(h_high, 1)

                for b in range(8):
                    if b < 7:
                        act.wait_ge(m1_full, i * 7 + (b + 1))
                    else:
                        act.wait_ge(w_used, i * 16 + (MLP_AT + KC))
                    act.activation(relu[:, b % 4, :], ps[:, b, :], ACT.Relu).then_inc(m1_out, 1)
                    if b:
                        high(b - 1)
                high(7)

        @block.vector
        def _(dve):
            dve.wait_ge(c_loaded, 16 * NCONST)
            def rows(t):
                if t >= 2:
                    dve.wait_ge(rowsT_done, 2 * (t - 1))
                dve.scalar_tensor_tensor(row[:, t % 2, :], x_in[:, t, :], rstd[:, t:t + 1], gain_row[:],
                                         ALU.mult, ALU.mult).then_inc(rows_ready, 1)
            for g in range(2):
                root_dve(dve, cols_of(4 * g, 4 * g + 4), D)
                for t in range(4 * g, 4 * g + 4):
                    rows(t)
                    if t:
                        low_rows(dve, 0, t - 1)
            low_rows(dve, 0, NT - 1)

            for t in range(NT):
                dve.wait_ge(sq_ready, t + 1)
                dve.tensor_reduce(hsum[:, t, 0:NHEADCOL],
                                  sq[:, t % 2, :].rearrange("p (h d) -> p h d", d=DK), AX, ALU.add).then_inc(sq_summed, 1)
            st = Steps(prep_step)
            st.mark(dve.tensor_scalar(qg[:], qg[:], DK ** -0.5, None, ALU.mult))
            dve.wait_ge(gates_exp, 1)
            st.mark(dve.tensor_scalar(gates[:, :, :], gates[:, :, :], 1.0, None, ALU.add))
            st.wait(dve)
            st.mark(dve.reciprocal(gates[:, :, :], gates[:, :, :]))
            st.wait(dve)
            g0 = gates[:, :, :].rearrange("p t (h b) -> p t h b", b=3)[:, :, :, 0]
            st.mark(dve.tensor_tensor(g0, g0, valid[:].unsqueeze(2).to_broadcast([P, NT, NH]), ALU.mult))
            root_dve(dve, head_bufs, DK)
            with dve.Fori(0, NT) as t:
                st.enter(t, 16)
                qv = nsa[:, bass.ds(t, 1), 0:KC0].rearrange("p a (h d) -> p (a h) d", d=DK)
                kv = nsa[:, bass.ds(t, 1), KC0:GT0].rearrange("p a (b c) -> p (a b) c", b=3)[:, :, 0:NG * DK]\
                    .rearrange("p b (g d) -> p b g d", d=DK)
                qr = hrstd[:, bass.ds(t, 1), 0:NH].rearrange("p a h -> p (a h)").unsqueeze(2).to_broadcast([P, NH, DK])
                kr = hrstd[:, bass.ds(t, 1), NH:20].rearrange("p a (b c) -> p (a b) c", c=4)[:, :, 0:NG]\
                    .unsqueeze(3).to_broadcast([P, 3, NG, DK])
                st.mark(dve.tensor_tensor(qv, qv, qr, ALU.mult))
                st.mark(dve.tensor_tensor(kv, kv, kr, ALU.mult))
                st.wait(dve)
                st.mark(dve.tensor_tensor(qv, qv, qg[:].unsqueeze(1).to_broadcast([P, NH, DK]), ALU.mult))
                st.mark(dve.tensor_tensor(kv, kv, kg[:].unsqueeze(1).unsqueeze(1).to_broadcast([P, 3, NG, DK]), ALU.mult))
                st.wait(dve)
                for part in range(2):
                    if part == 0:
                        ra, rb = qv[:, :, 0:8], qv[:, :, 8:16]
                        co, si = (rope[:, bass.ds(t, 1), 8 * i:8 * i + 8].to_broadcast([P, NH, 8]) for i in range(2))
                        tm = [rtmp[:, i, 0:64].rearrange("p (h e) -> p h e", e=8) for i in range(4)]
                    else:
                        ra, rb = kv[:, :, :, 0:8], kv[:, :, :, 8:16]
                        co, si = (rope[:, bass.ds(t, 1), 8 * i:8 * i + 8].unsqueeze(1).to_broadcast([P, 3, NG, 8]) for i in range(2))
                        tm = [rtmp[:, i, 64:112].rearrange("p (b g e) -> p b g e", g=NG, e=8) for i in range(4)]
                    for i, (u, v_) in enumerate(((ra, co), (rb, si), (rb, co), (ra, si))):
                        st.mark(dve.tensor_tensor(tm[i], u, v_, ALU.mult))
                    st.wait(dve)
                    st.mark(dve.tensor_tensor(ra, tm[0], tm[1], ALU.subtract))
                    st.mark(dve.tensor_tensor(rb, tm[2], tm[3], ALU.add))
                st.wait(dve)
            st.leave(NT)
            dve.tensor_copy(qg[:, 0:1], qg[:, 0:1]).then_inc(prep_done, 1)

            hs = Steps(hid_step)
            dve.wait_ge(smallT_out, 2)
            hs.mark(dve.tensor_tensor(lb[:, 4, :], lb[:, 0, :], lb[:, 1, :], ALU.max))
            hs.wait(dve)
            hs.mark(dve.tensor_tensor(lb[:, 2, :], lb[:, 0, :], lb[:, 4, :], ALU.subtract))
            hs.mark(dve.tensor_tensor(lb[:, 3, :], lb[:, 1, :], lb[:, 4, :], ALU.subtract))
            dve.wait_ge(lb_exp, 1)
            hs.mark(dve.tensor_tensor(lb[:, 4, :], lb[:, 2, :], lb[:, 3, :], ALU.add))
            hs.wait(dve)
            hs.mark(dve.reciprocal(lb[:, 4, :], lb[:, 4, :]))
            hs.wait(dve)
            hs.mark(dve.tensor_tensor(lb[:, 0, :], lb[:, 2, :], lb[:, 4, :], ALU.mult))
            hs.wait(dve)
            hs.mark(dve.tensor_scalar(lb[:, 1, :], lb[:, 0, :], -1.0, 1.0, ALU.mult, ALU.add))
            for kv in range(2):
                for b in range(2):
                    dve.wait_ge(tokT_done, 2 * kv + b + 1)
                    if kv and not b:
                        dve.wait_ge(hid_full, 1)
                    for half in range(2):
                        pe16 = peT[:, kv, 16 * half:16 * half + 16].unsqueeze(1).to_broadcast([P, BW // 16, 16])
                        dve.tensor_tensor(kcab[:, half, b * BW:(b + 1) * BW].rearrange("p (n j) -> p n j", j=16),
                                          ps[:, 1 + 2 * kv + b, :].rearrange("p (n j) -> p n j", j=16), pe16, ALU.add)\
                            .then_inc(tok_pe, 1)
                if kv == 0:
                    dve.wait_ge(tokT_done, 4)
                    hs.mark(dve.memset(hid2, 0.0))
                dve.wait_ge(hid_exp, kv + 1)
                hs.mark(dve.tensor_scalar(hid_e, hid_e, 1.0, None, ALU.add))
                hs.wait(dve)
                hs.mark(dve.reciprocal(hid_e, hid_e))
                hs.wait(dve)
                if kv:
                    dve.wait_ge(cmp_full, 1)
                dve.tensor_tensor(hid2.rearrange("p (g a n) -> p g a n", g=NG, a=2)[:, :, :, 0:NCMP],
                                  hid_ps.unsqueeze(2).to_broadcast([P, NG, 2, NCMP]),
                                  hid_e.unsqueeze(2).to_broadcast([P, NG, 2, NCMP]), ALU.mult).then_inc(hid_ready, 1)
                if kv == 0:
                    dve.wait_ge(cmp_high, 1)
                    dve.tensor_tensor(kc_L[:, :, :].rearrange("p g n -> p (g n)"), ps[:, 0, 0:P],
                                      kc_H[:, :, :].rearrange("p g n -> p (g n)").bitcast(F32), ALU.subtract).then_inc(cmp_low, 1)

            pr = Steps(pre_step)
            for n in range(8):
                e = pre_e[n % 2]
                dve.wait_ge(pre_exp, n + 1)
                pr.mark(dve.tensor_scalar(e, e, 1.0, None, ALU.add))
                pr.wait(dve)
                pr.mark(dve.reciprocal(e, e))
                pr.wait(dve)
                if n < 4:
                    dve.tensor_tensor(pre_x[n], pre_x[n], e, ALU.mult).then_inc(pre_done, 1)
                else:
                    for c in range(2):
                        x3 = pre_x[n][:, c * BW:(c + 1) * BW].rearrange("p (h t) -> p h t", t=P)
                        e3 = e[:, c * BW:(c + 1) * BW].rearrange("p (h t) -> p h t", t=P)
                        pr.mark(dve.tensor_tensor(x3, e3, lb[:, 1, :].unsqueeze(2).to_broadcast([P, HH, P]), ALU.mult))
                        pr.wait(dve)
                        ins = dve.tensor_tensor(x3, x3, lb[:, 0, :].unsqueeze(2).to_broadcast([P, HH, P]), ALU.add)
                        ins.then_inc(pre_done, 1) if c else pr.mark(ins)

            for m in range(8):
                dve.wait_ge(t_act, m + 1)
                dve.tensor_tensor(key_stack(KS_L, m), ps[:, 4 + m % 2, :], key_stack(KS_H, m).bitcast(F32),
                                  ALU.subtract).then_inc(t_dve, 1)
            at_ = Steps(att_step)

            def att_dve(g, pr):
                i = g * 2 + pr
                tb, ab, vb, ib = i * len(it.groups) + 8, i * it.n_act + 8, i * it.n_dve + 8, i * len(it.items)

                def prep(hh):
                    for half, m in enumerate(it.prep[hh]):
                        dve.wait_ge(t_act, ab + it.groups[m]["act_after"])
                        q = QT[DK:P, hh, half * BW:(half + 1) * BW]
                        dve.tensor_tensor(q, ps[DK:P, 4 + m % 2, :], q.bitcast(F32), ALU.subtract).then_inc(t_dve, 1)

                def maximum(j):
                    kind, hh, t, tiles = it.items[j]
                    dve.wait_ge(qk_done, ib + (j + 1))
                    if kind != "cmp":
                        sv = scores_view(j)
                        dve.tensor_reduce(negmax[:, j:j + 1], sv, AX if len(sv.shape) == 2 else mybir.AxisListType.XY,
                                          ALU.max, negate=True).then_inc(max_done, 1)
                        return
                    sv = ps[:, 2 * (j % 2), :].rearrange("p (t n) -> p t n", n=NCP)
                    at_.mark(dve.tensor_reduce(cmx[:, 0, :], sv, AX, ALU.max))
                    at_.wait(dve)
                    dve.tensor_tensor(cdiff[:].rearrange("p (t n) -> p t n", n=NCP), sv,
                                      cmx[:, 0, :].unsqueeze(2).to_broadcast([P, NT, NCP]), ALU.subtract).then_inc(max_done, 1)

                def finalize(j):
                    kind, hh, t, tiles = it.items[j]
                    head3 = g * 12 + pr * 6 + 3 * hh
                    ycol = g * 256 + pr * 128 + hh * DK
                    bank = 6 + it.alloc(j) % 2
                    if kind == "slc":
                        return
                    if kind == "cmp":
                        y = nsa[:, :, bass.ds(ycol, DK)]
                        at_.mark(dve.reciprocal(cmx[:, 2, :], cmx[:, 1, :]))
                        at_.wait(dve)
                        at_.mark(dve.tensor_tensor(cmx[:, 2, :], cmx[:, 2, :],
                                                   gates[:, :, bass.ds(head3, 1)].rearrange("p t a -> p (t a)"), ALU.mult))
                        at_.wait(dve)
                        dve.wait_ge(pv_done, ib + (j + 1))
                        dve.tensor_tensor(y, ps[:, bank, :].rearrange("p (t d) -> p t d", d=DK),
                                          cmx[:, 2, :].unsqueeze(2).to_broadcast([P, NT, DK]), ALU.mult).then_inc(o_free, 1)
                        return
                    y = nsa[:, t, bass.ds(ycol, DK)]
                    c = coef[:, hh, t, :]
                    dve.wait_ge(exp_done, ib + (j + 1))
                    at_.mark(dve.reciprocal(c, rsums[:, hh, t, :]))
                    at_.wait(dve)
                    at_.mark(dve.tensor_tensor(c, c, gates[:, t, bass.ds(head3 + 1, 2)], ALU.mult))
                    at_.wait(dve)
                    dve.wait_ge(pv_done, ib + (j + 1))
                    dve.wait_ge(o_free, i * 18 + (hh * 9 + 1 + t))
                    at_.mark(dve.scalar_tensor_tensor(y, ps[:, bank, 0:DK], coef[:, hh, t, 0:1], y, ALU.mult, ALU.add))
                    at_.wait(dve)
                    dve.scalar_tensor_tensor(y, ps[:, bank, DK:2 * DK], coef[:, hh, t, 1:2], y, ALU.mult, ALU.add)\
                        .then_inc(o_free, 1)

                prep(0)
                maximum(0)
                for j in range(len(it.items)):
                    if j == PREP_AT:
                        prep(1)
                    if j + 1 < len(it.items):
                        maximum(j + 1)
                    kind, hh, t, tiles = it.items[j]
                    if kind == "cmp":
                        dve.wait_ge(exp_done, ib + (j + 1))
                        dve.tensor_reduce(cmx[:, 1, :], probs[:, j % 2, 0:BW].rearrange("p (t n) -> p t n", n=NCP),
                                          AX, ALU.add).then_inc(csum_done, 1)
                    for m in it.of[j]:
                        if it.groups[m]["dve"]:
                            dve.wait_ge(t_full, tb + (m + 1))
                            pt_free(dve, m, ib)
                            n = it.groups[m]["n"] * P
                            dve.tensor_copy(pT[:, it.groups[m]["pt"], 0:n], ps[:, 4 + m % 2, 0:n]).then_inc(t_dve, 1)
                    if j:
                        if it.items[j - 1][0] == "cmp":
                            dve.wait_ge(csum_done, i * 2 + (it.items[j - 1][1] + 1))
                        finalize(j - 1)
                finalize(len(it.items) - 1)

            with dve.Fori(0, NG) as g:
                with dve.Fori(0, 2) as pr:
                    at_.enter(g * 2 + pr, 2 * (3 + 3 * NT))
                    att_dve(g, pr)
            at_.leave(4)

            dve.wait_ge(fill_set, 5)
            dve.wait_ge(t_full, 8 + 4 * len(it.groups))
            dve.memset(hst[:], 0.0).then_inc(st_ready, 1)
            for n in range(4):
                f2 = fm[:, 1, 2 * n:2 * n + 2, :, :].rearrange("p c h t -> p (c h t)")
                dve.wait_ge(ln_done, n + 1)
                dve.wait_ge(k_done, n + 1)
                dve.tensor_tensor_scan(f2, hone[:], hlf[:, n % 2, :], 0.0, ALU.mult, ALU.add).then_inc(bc_done, 1)
            dve.wait_ge(bc_done, 4)
            dve.wait_ge(t_loaded, 16)
            sst = Steps(st_step)
            with dve.Fori(0, NT) as c:
                sst.enter(c, HH - 1)
                q_c = fm[:, 0, bass.ds(c, 1), :, :].rearrange("p a h t -> p (a h t)")

                def merge(u):
                    dve.wait_ge(A_full, c * 8 + (u + 1))
                    if u:
                        dve.wait_ge(A_merged, c * 8 + u)
                    stand_alone(dve)
                    dve.copy_predicated(per_head(hA[:]), tree[:, u, :].unsqueeze(1).to_broadcast([P, HH, P]),
                                        per_head(ps[:, u % 2, :])).then_inc(A_merged, 1)

                dve.wait_ge(st_ready, c + 1)
                for n, b in enumerate(LEVELS):
                    dve.wait_ge(e_half, c * 7 + (n + 1))
                    if n >= 2:
                        dve.wait_ge(A_full, c * 8 + (n - 1))
                    dve.tensor_tensor(tree_halves(hQ[:, n % 2, :], b)[1], tree_halves(q_c, b)[1],
                                      tree_halves(hE[:, n % 2, :], b)[1], ALU.mult).then_inc(q_ready, 1)
                    if n:
                        merge(n - 1)
                dve.wait_ge(eb_ready, c + 1)
                dve.tensor_tensor(hQe[:], q_c, hEe[:, 0, :], ALU.mult).then_inc(qe_ready, 1)
                merge(6)
                merge(7)
                dve.wait_ge(st_full, c + 1)
                for h in range(HH):
                    cols = slice(h * P, (h + 1) * P)
                    ins = dve.scalar_tensor_tensor(hst[:, cols], hst[:, cols], hEe[:, 0, (h + 1) * P - 1:(h + 1) * P],
                                                   ps[:, 4, cols], ALU.mult, ALU.add)
                    ins.then_inc(st_ready, 1) if h == HH - 1 else sst.mark(ins)
            sst.leave(NT)

            mx = Steps(mix_step)
            dve.wait_ge(g_loaded, 32)
            for t in range(NT):
                dve.wait_ge(osq_ready, t + 1)
                dve.tensor_reduce(ssq[:, NT + HH * t:NT + HH * (t + 1)], per_head(osq[t % 2]), AX, ALU.add)\
                    .then_inc(osq_summed, 1)
                dve.wait_ge(eg_ready, t + 1)
                mx.mark(dve.tensor_scalar(eg[t % 2], eg[t % 2], 1.0, None, ALU.add))
                mx.wait(dve)
                mx.mark(dve.reciprocal(eg[t % 2], eg[t % 2]))
                gt = hv[:, 1, t, :]
                mx.mark(dve.tensor_tensor(per_head(gt), per_head(gt), hgain.unsqueeze(1).to_broadcast([P, HH, P]), ALU.mult))
                mx.wait(dve)
                dve.tensor_tensor(gt, gt, eg[t % 2], ALU.mult).then_inc(mg_ready, 1)
            root_dve(dve, cols_of(0, NT), BW)
            root_dve(dve, cols_of(NT, NT + NT * HH), P)
            dve.wait_ge(mg_ready, NT)
            for t in range(NT):
                if t >= 2:
                    dve.wait_ge(rowsT_done, 16 + 2 * (t - 1))
                o = hv[:, 0, t, :]
                mx.mark(dve.tensor_tensor(per_head(o), per_head(o), rstd[:, NT + HH * t:NT + HH * (t + 1)].unsqueeze(2)
                                          .to_broadcast([P, HH, P]), ALU.mult))
                mx.mark(dve.scalar_tensor_tensor(row2[:, t % 2, 0:BW], nsa[:, t, 0:BW], rstd[:, t:t + 1], ngain,
                                                 ALU.mult, ALU.mult))
                mx.wait(dve)
                dve.tensor_tensor(row2[:, t % 2, BW:D], o, hv[:, 1, t, :], ALU.mult).then_inc(rows_ready, 1)
                if t:
                    low_rows(dve, 1, t - 1)
            low_rows(dve, 1, NT - 1)

            def add_banks(full, count, used, half):
                for t in range(NT):
                    if t < 7:
                        dve.wait_ge(full, count + (t + 1))
                    else:
                        dve.wait_ge(w_used, used)
                    xs = x1[:, t, half * BW:(half + 1) * BW]
                    dve.tensor_tensor(xs, ps[:, t, :], xs, ALU.add).then_inc(res_out, 1)

            dve.wait_ge(x2_loaded, 16 * NT)
            for half in range(2):
                add_banks(wo_full, 7 * half, W_OUT_AT + KC * (half + 1), half)

            dve.wait_ge(g2_loaded, 16)
            for g in range(2):
                root_dve(dve, cols_of(48 + 4 * g, 52 + 4 * g), D)
                for t in range(4 * g, 4 * g + 4):
                    if t < 2:
                        dve.wait_ge(rowsT_done, 32)
                    else:
                        dve.wait_ge(rowsT_done, 32 + 2 * (t - 1))
                    dve.scalar_tensor_tensor(row2[:, t % 2, :], x1[:, t, :], rstd[:, 48 + t:49 + t], gain2[:],
                                             ALU.mult, ALU.mult).then_inc(rows_ready, 1)
                    if t:
                        low_rows(dve, 2, t - 1)
            low_rows(dve, 2, NT - 1)

            with dve.Fori(0, NF) as i:
                def low(b):
                    dve.wait_ge(h_high, i * 8 + (b + 1))
                    c, half = divmod(b, 2)
                    cols = slice(half * BW, (half + 1) * BW)
                    dve.tensor_tensor(h1_L[:, c, cols], relu2[:, b % 4, :], h1_H[:, c, cols].bitcast(F32), ALU.subtract)\
                        .then_inc(h_low, 1)

                for b in range(8):
                    dve.wait_ge(m1_out, i * 8 + (b + 1))
                    dve.tensor_tensor(relu2[:, b % 4, :], relu[:, b % 4, :], relu[:, b % 4, :], ALU.mult).then_inc(sqd, 1)
                    if b:
                        low(b - 1)
                low(7)
                for half in range(2):
                    add_banks(m2_full, i * 14 + 7 * half, i * 16 + (MLP_AT + KC + 4 * (half + 1)), half)

        @block.tensor
        def _(pe):
            pe.wait_ge(c_loaded, 16 * NCONST)
            for t in range(NT):
                transpose_rows(pe, 0, t, row)

            def compress_pe(pe):
                pe.wait_ge(proj_out, 40)
                for kv in range(2):
                    nc.tensor.transpose(ps[:, 0, kv * CMP_LEN:(kv + 1) * CMP_LEN], pe_sb[:, kv, :, :].rearrange("j a d -> j (a d)"),
                                        eye[0:CMP_LEN, 0:CMP_LEN])
                nc.tensor.transpose(ps[:, 0, 64:64 + 2 * HH], lb_rows[:], eye[0:2 * HH, 0:2 * HH]).then_inc(smallT, 1)
                pe.wait_ge(prep_done, 1)
                for kv in range(2):
                    for t in range(NT):
                        ins = nc.tensor.transpose(ps[:, 1 + 2 * kv + t // 4, (t % 4) * P:(t % 4 + 1) * P],
                                                  nsa[:, t, KC0 + kv * P:KC0 + (kv + 1) * P], eye[:])
                        if t % 4 == 3:
                            ins.then_inc(tokT_done, 1)
                pe.wait_ge(c2_loaded, 64)
                for kv in range(2):
                    pe.wait_ge(tok_pe, 4 * (kv + 1))
                    if kv:
                        pe.wait_ge(hid_ready, 1)
                    for j in range(CMP_LEN):
                        for g in range(NG):
                            rows = slice(g * DK, (g + 1) * DK)
                            half, jj = divmod(j, 16)
                            off = 16 * half + jj
                            ins = nc.tensor.matmul(ps[:, 5 + g, 0:NCMP], w1[rows, kv, j, :],
                                                   kcab[rows, half, off:off + 16 * (NCMP - 1) + 1:16],
                                                   start=j == 0, stop=j == CMP_LEN - 1)
                    ins.then_inc(hid_full, 1)
                    pe.wait_ge(hid_ready, kv + 1)
                    h2 = hid2.rearrange("p (g a n) -> p g a n", g=NG, a=2)
                    if kv == 0:
                        nc.tensor.matmul(ps[:, 0, 0:P].rearrange("p (g n) -> p g n", g=NG), w2[:, 0, :, :].rearrange("p a d -> p (a d)"),
                                         h2[:, :, 0, :], start=True, stop=True).then_inc(cmp_full, 1)
                    else:
                        for g in range(NG):
                            ins = nc.tensor.matmul(ps[:, 7, g * DK:(g + 1) * DK], h2[:, g, :, :].rearrange("p a n -> p (a n)"),
                                                   w2[:, 1, 0, :], start=True, stop=True)
                        ins.then_inc(cmp_full, 1)
                pe.wait_ge(cmp_high, 3)
                pe.wait_ge(cmp_low, 1)

            pe.wait_ge(rows_low, 2 * NT)
            for j in range(KC):
                rows_chunk(pe, 0, j, TAIL, proj_full)

            def freed(blk):
                return lambda b: pe.wait_ge(proj_out, (blk - 1) * 8 + (b + 1))

            for pair in range(3):
                if pair == 2:
                    compress_pe(pe)
                with pe.Fori(0, 2) as i:
                    blk = i + (1 + 2 * pair)
                    for j in range(KC):
                        if pair == 1:
                            cols_chunk(pe, blk * KC, j, proj_full, freed(blk))
                        else:
                            rows_chunk(pe, blk * KC, j, BW, proj_full, freed(blk))

            pe.wait_ge(proj_out, 8 * len(blocks))
            for m in range(8):
                n, half = divmod(m, 2)
                if half == 0:
                    pe.wait_ge(stage_ready, n + 1)
                if m >= 2:
                    pe.wait_ge(t_dve, m - 1)
                stack_half(pe, m, n % 2, half)
            pe.wait_ge(m_loaded, 32)

            def att_pe(g, pr):
                i = g * 2 + pr
                ab, vb, ib = i * it.n_act + 8, i * it.n_dve + 8, i * len(it.items)

                def bank_free(m):
                    if m < 2:
                        pe.wait_ge(t_act, ab)
                        pe.wait_ge(t_dve, vb)
                        return
                    u = it.groups[m - 2]
                    if u["act"]:
                        pe.wait_ge(t_act, ab + u["act_after"])
                    if u["dve"]:
                        pe.wait_ge(t_dve, vb + u["dve_after"])

                def prep(hh):
                    pe.wait_ge(stage_ready, i * 2 + (4 + hh + 1))
                    for half, m in enumerate(it.prep[hh]):
                        bank_free(m)
                        stack_half(pe, m, hh, half)

                def scores(j):
                    kind, hh, t, tiles = it.items[j]
                    s_ = 2 * (j % 2)
                    if kind == "cmp":
                        pe.wait_ge(t_dve, vb + it.groups[it.prep[hh][1]]["dve_after"])
                        nc.tensor.matmul(ps[:, s_, :], masks[:, 0:P], cmask[:], start=True, stop=False, skip_group_check=True)
                        for t in range(NT):
                            o = ps[:, s_, t * NCP:(t + 1) * NCP]
                            for k_ in (kc_H, kc_L):
                                ins = nc.tensor.matmul(o, QT[:, hh, t * P:(t + 1) * P],
                                                       k_[:, bass.ds(g, 1), :].rearrange("p a n -> p (a n)"),
                                                       start=False, stop=t == NT - 1 and k_ is kc_L, skip_group_check=True)
                        ins.then_inc(qk_done, 1)
                        return
                    br = int(kind == "win")
                    w = max(2, len(tiles)) * P
                    nb = 1 if w <= BW else 2
                    mask_at = {(nb - 1, len(tiles) * P // nb - P): 1}
                    if br and t >= WIN_T:
                        mask_at[(0, 0)] = 2
                    ms = [(b, c, k) for (b, c), k in mask_at.items()]
                    for b in range(nb):
                        o = ps[:, s_ + b, 0:w // nb]
                        mine = [(c, k) for bb, c, k in ms if bb == b]
                        for n, k_ in enumerate((KS_H, KS_L)):
                            ins = nc.tensor.matmul(o, QT[:, hh, t * P:(t + 1) * P],
                                                   k_[:, br, bass.ds(g, 1), tiles[0] * P + b * (w // nb):tiles[0] * P + (b + 1) * (w // nb)]
                                                   .rearrange("p a n -> p (a n)"),
                                                   start=n == 0, stop=n == 1 and not mine, skip_group_check=True)
                        for q, (c, k) in enumerate(mine):
                            ins = nc.tensor.matmul(ps[:, s_ + b, c:c + P], masks[:, 0:P], masks[:, k * P:(k + 1) * P],
                                                   start=False, stop=q == len(mine) - 1, skip_group_check=True)
                    ins.then_inc(qk_done, 1)

                def transposes(j):
                    pe.wait_ge(exp_done, ib + (j + 1))
                    for m in it.of[j]:
                        bank_free(m)
                        u = it.groups[m]
                        for q in range(u["n"]):
                            ins = nc.tensor.transpose(ps[:, 4 + m % 2, q * P:(q + 1) * P],
                                                      probs[:, j % 2, (u["first"] + q) * P:(u["first"] + q + 1) * P], eye[:])
                        ins.then_inc(t_full, 1)

                def outputs(j):
                    kind, hh, t, tiles = it.items[j]
                    a = it.alloc(j)
                    if kind != "win" and a >= 2:
                        pe.wait_ge(o_free, i * 18 + (a - 1))
                    for m in it.of[j]:
                        u = it.groups[m]
                        if u["act"]:
                            pe.wait_ge(t_act, ab + u["act_after"])
                        else:
                            pe.wait_ge(t_dve, vb + u["dve_after"])
                        for q in range(u["n"]):
                            lhs = pT[:, u["pt"], q * P:(q + 1) * P]
                            if kind == "cmp":
                                for half in range(2):
                                    t2 = 2 * q + half
                                    ins = nc.tensor.matmul(ps[:, 6 + a % 2, t2 * DK:(t2 + 1) * DK], lhs,
                                                           vc[:, half, bass.ds(g, 1), :].rearrange("p a d -> p (a d)"),
                                                           start=True, stop=True)
                            else:
                                n = u["first"] + q
                                c, v0 = (DK, VW0) if kind == "win" else (0, VS0)
                                ins = nc.tensor.matmul(ps[:, 6 + a % 2, c:c + DK], lhs, nsa[:, tiles[n], bass.ds(g * DK + v0, DK)],
                                                       start=n == 0, stop=n == len(tiles) - 1)
                    ins.then_inc(pv_done, 1)

                prep(0)
                scores(0)
                for j in range(len(it.items)):
                    if j == PREP_AT:
                        prep(1)
                    if j + 1 < len(it.items):
                        scores(j + 1)
                    transposes(j)
                    if j:
                        outputs(j - 1)
                outputs(len(it.items) - 1)

            with pe.Fori(0, NG) as g:
                with pe.Fori(0, 2) as pr:
                    att_pe(g, pr)

            pe.wait_ge(bc_done, 4)
            with pe.Fori(0, NT) as c:
                def product(u, lhs, rhs):
                    for h in range(HH):
                        ins = nc.tensor.matmul(ps[:, u % 2, h * P:(h + 1) * P], lhs(h), rhs(h), start=True, stop=True)
                    ins.then_inc(A_full, 1)

                for n in range(len(LEVELS)):
                    pe.wait_ge(q_ready, c * 7 + (n + 1))
                    pe.wait_ge(kk_ready, c * 7 + (n + 1))
                    if n >= 2:
                        pe.wait_ge(A_merged, c * 8 + (n - 1))
                    product(n, lambda h: hK[:, n % 2, h * P:(h + 1) * P], lambda h: hQ[:, n % 2, h * P:(h + 1) * P])
                pe.wait_ge(k0_ready, c + 1)
                pe.wait_ge(A_merged, c * 8 + 6)
                product(7, lambda h: hK0[:, h * P:(h + 1) * P],
                        lambda h: fm[:, 0, bass.ds(c, 1), h, :].rearrange("p a t -> p (a t)"))
                pe.wait_ge(kd_ready, c + 1)
                for h in range(HH):
                    ins = nc.tensor.transpose(ps[:, 3, h * P:(h + 1) * P], hKd[:, h * P:(h + 1) * P], eye[:])
                ins.then_inc(KT_full, 1)
                pe.wait_ge(KT_ready, c + 1)
                pe.wait_ge(qe_ready, c + 1)
                pe.wait_ge(A_merged, c * 8 + 8)
                pe.wait_ge(st_ready, c + 1)
                v = [hv[:, 0, bass.ds(c, 1), h * P:(h + 1) * P].rearrange("p a x -> p (a x)") for h in range(HH)]
                for h in range(HH):
                    cols = slice(h * P, (h + 1) * P)
                    nc.tensor.matmul(ps[:, 2, cols], hA[:, cols], v[h], start=True, stop=False)
                    nc.tensor.matmul(ps[:, 2, cols], hQe[:, cols], hst[:, cols], start=False, stop=True)
                for h in range(HH):
                    cols = slice(h * P, (h + 1) * P)
                    ins = nc.tensor.matmul(ps[:, 4, cols], hKT[:, cols], v[h], start=True, stop=True)
                ins.then_inc(st_full, 1)

            for t in range(NT):
                transpose_rows(pe, 1, t, row2)
            pe.wait_ge(rows_low, 32)
            for j in range(16):
                rows_chunk(pe, W_OUT_AT, j, BW, wo_full,
                           (lambda b: pe.wait_ge(res_out, b + 1)) if j >= KC else None)

            pe.wait_ge(res_out, 16)
            for t in range(NT):
                transpose_rows(pe, 2, t, row2)
            pe.wait_ge(rows_low, 48)

            with pe.Fori(0, NF) as i:
                n = i * 16 + MLP_AT
                for j in range(KC):
                    cols_chunk(pe, n, j, m1_full, lambda b: pe.wait_ge(res_out, i * 16 + (8 + b + 1)))
                for j in range(KC):
                    half, fc = divmod(j, 4)
                    s_ = (KC + j) % RING
                    pe.wait_ge(w_split, n + (KC + j + 1))
                    if half == 0:
                        pe.wait_ge(h_low, i * 8 + (2 * fc + 2))
                    for t in range(NT):
                        if fc == 0:
                            if half == 0:
                                pe.wait_ge(m1_out, i * 8 + (t + 1))
                            else:
                                pe.wait_ge(res_out, i * 16 + (16 + t + 1))
                        a = [h[:, fc, t * P:(t + 1) * P] for h in (h1_H, h1_L)]
                        r = [w[:, s_, :] for w in (w_high, w_low)]
                        ins = three_passes(ps[:, t, :], a, r, fc == 0, fc == 3)
                        if t == 7:
                            ins.then_inc(w_used, 1)
                        elif fc == 3:
                            ins.then_inc(m2_full, 1)


_INS = ["x", "attn_norm", "w_in", "q_norm", "k_norm", "cmp_pe_k", "cmp_w1_k", "cmp_w2_k", "cmp_pe_v", "cmp_w1_v",
        "cmp_w2_v", "nsa_out_norm", "hgrn_lb", "hgrn_out_norm", "w_out", "mlp_norm", "w_mlp_in", "w_mlp_out"]


def kernel(**inputs):
    import numpy as _np
    import concourse.bacc as _bacc
    from concourse import mybir as _mybir
    from concourse.bass_utils import run_bass_kernel_spmd as _run

    nc = _bacc.Bacc("TRN2", target_bir_lowering=False, num_devices=1)
    arrays, args = {}, []
    data = {name: _np.ascontiguousarray(inputs[name]) for name in _INS}
    data.update(constants())
    for name, a in data.items():
        arrays[f"in_{name}_dram"] = a
        args.append(nc.dram_tensor(f"in_{name}_dram", a.shape, _mybir.dt.from_np(a.dtype), kind="ExternalInput").ap())
    out = nc.dram_tensor("out_0_dram", (1, S, D), _mybir.dt.float32, kind="ExternalOutput").ap()
    program(nc, *args, out)
    r = _run(nc, [arrays], core_ids=[0])
    return r.results[0]["out_0_dram"]
```

```python
import numpy as np
import concourse.bass as bass
from concourse import mybir

F32 = mybir.dt.float32
F32R = mybir.dt.float32r
BF16 = mybir.dt.bfloat16
I32 = mybir.dt.int32
ALU = mybir.AluOpType
ACT = mybir.ActivationFunctionType
AX = mybir.AxisListType.X

P = 128
S = 1024
D = 1024
NT = S // P
KC = D // P
NH, NG, DK = 8, 2, 64
HPG = NH // NG
CMP_LEN, CMP_STRIDE = 32, 16
NCMP = (S - CMP_LEN) // CMP_STRIDE + 1
NCP = NCMP + 1
CMP_STEPS = CMP_LEN // 2
WIN_T = 512 // P
HH = 4
FF = 4096
BW = 512
EPS = 1e-6
NEG = -1e30
Q0, KC0, VC0, KS0, VS0, KW0, VW0, GT0 = 0, 512, 640, 768, 896, 1024, 1152, 1280
NSAW = 1304
HQ0, HI0 = NSAW, NSAW + 1024
NHEADCOL = KW0 // DK + NG
TAIL = NSAW - 2 * BW
LEVELS = [64, 32, 16, 8, 4, 2, 1]
NF = FF // BW


def as_bf16(a):
    return np.ascontiguousarray((a.view(np.uint32) >> 16).astype(np.uint16))


def constants():
    pos = np.arange(S, dtype=np.float32)
    inv = (np.float32(500000.0) ** (-np.arange(0, 16, 2, dtype=np.float32) / np.float32(16))).astype(np.float32)
    ang = (pos[:, None] * inv[None, :]).astype(np.float32)
    rope = np.concatenate([np.cos(ang), np.sin(ang)], axis=1).astype(np.float32)
    i = np.arange(P)
    eye = np.eye(P, dtype=np.float32)
    masks = np.zeros((P, 3 * P), np.float32)
    masks[:, 0:P] = eye
    masks[:, P:2 * P] = np.where(i[None, :] <= i[:, None], 0.0, NEG)
    masks[:, 2 * P:] = np.where(i[None, :] > i[:, None], 0.0, NEG)
    t = (np.arange(NT)[:, None] * P + i[None, :])
    end = np.arange(NCP) * CMP_STRIDE + CMP_LEN - 1
    ok = (end[None, None, :] <= t[:, :, None]) & (np.arange(NCP) < NCMP)[None, None, :]
    cmask = np.where(ok, 0.0, NEG).transpose(1, 0, 2).reshape(P, NT * NCP).astype(np.float32)
    valid = (t >= CMP_LEN - 1).T.astype(np.float32)
    tree = np.zeros((P, (len(LEVELS) + 1) * P), np.int32)
    for n, b in enumerate(LEVELS):
        same = (i[:, None] // (2 * b)) == (i[None, :] // (2 * b))
        tree[:, n * P:(n + 1) * P] = same & (i[:, None] % (2 * b) < b) & (i[None, :] % (2 * b) >= b)
    tree[:, len(LEVELS) * P:] = np.eye(P)
    return {"c_rope": rope, "c_eye": eye, "c_masks": as_bf16(masks), "c_cmask": as_bf16(cmask),
            "c_valid": np.ascontiguousarray(valid), "c_tree": tree}


class Steps:

    def __init__(self, sem):
        self.sem, self.base, self.n = sem, 0, 0

    def mark(self, ins):
        self.n += 1
        return ins.then_inc(self.sem, 1)

    def now(self):
        return self.base + self.n

    def wait(self, eng):
        eng.wait_ge(self.sem, self.now())

    def enter(self, trip, per):
        self.start, self.per = self.base + self.n, per
        self.base, self.n = trip * per + self.start, 0

    def leave(self, trips):
        assert self.n == self.per, (self.n, self.per)
        self.base, self.n = self.start + trips * self.per, 0


class Items:

    def __init__(self):
        self.items = []
        for hh in range(2):
            self.items.append(("cmp", hh, 0, []))
            for t in range(NT):
                self.items.append(("slc", hh, t, list(range(t + 1))))
                self.items.append(("win", hh, t, list(range(max(0, t - WIN_T), t + 1))))
        self.per_head = len(self.items) // 2
        self.groups, self.of = [], {}
        self.prep = {}
        self.order = []
        out = {}
        for j in range(len(self.items)):
            if j == NEXT_AT:
                self._prep(0)
            elif j == PREP_AT:
                self._prep(1)
            kind, hh, t, tiles = self.items[j]
            n = 4 if kind == "cmp" else len(tiles)
            self.of[j] = []
            for g0 in range(0, n, 4):
                self.of[j].append(len(self.groups))
                self.groups.append(dict(item=j, first=g0, n=min(4, n - g0)))
        use_a = use_v = use_pt = 0
        for m, g in enumerate(self.groups):
            if g["item"] is None:
                g["act"], g["dve"] = True, True
            else:
                g["act"] = m % 2 == 0 or g["n"] <= 1
                g["dve"] = not g["act"]
                g["pt"] = use_pt % PT_SLOTS
                g["ptn"] = use_pt
                use_pt += 1
            use_a += g["act"]
            use_v += g["dve"]
            g["act_after"], g["dve_after"] = use_a, use_v
        self.n_act, self.n_dve, self.n_pt = use_a, use_v, use_pt
        self.place()
        assert use_pt % PT_SLOTS == 0 and len(self.groups) % 2 == 0

    def place(self):
        last = [-1] * S_BANKS
        self.banks, self.before = [], []
        for j, (kind, _, _, tiles) in enumerate(self.items):
            choices = [[b] for b in range(S_BANKS)] if len(tiles) <= 4 else [[b, b + 1] for b in range(S_BANKS - 1)]
            mine = min(choices, key=lambda c: (any(self.output_near(last[b], j) for b in c), max(last[b] for b in c)))
            self.banks.append(mine)
            self.before.append([last[b] for b in mine if last[b] >= 0])
            for b in mine:
                last[b] = j

    def output_near(self, u, j):
        near = u >= 0 and self.items[u][0] == "cmp" and j < u + AHEAD + 3
        return near

    def pair(self, j):
        hh, k = divmod(j, self.per_head)
        return NT * hh + (k - 1) // 2

    def pair_end(self, n):
        return (NT + 1) * (n // NT) + 2 + n % NT

    def _prep(self, hh):
        self.prep[hh] = [len(self.groups), len(self.groups) + 1]
        for half in range(2):
            self.groups.append(dict(item=None, hh=hh, half=half, n=4))


PREP_AT = 9
NEXT_AT = 27
FIRST = 10
PT_SLOTS = 10
P_SLOTS = 4
AHEAD = 3
S_BANKS = 4
T_BANK = 4
O_BANK = 6
D_SLOTS, E_SLOTS, X_SLOTS = 4, 3, 4
A_BANKS = (0, 1, 5, 6)


def program(nc, x, attn_norm, w_in, q_norm, k_norm, cmp_pe_k, cmp_w1_k, cmp_w2_k, cmp_pe_v, cmp_w1_v,
            cmp_w2_v, nsa_out_norm, hgrn_lb, hgrn_out_norm, w_out, mlp_norm, w_mlp_in, w_mlp_out,
            c_rope, c_eye, c_masks, c_cmask, c_valid, c_tree, out):
    at = {"small": 197376}
    base = (nc.sbuf_base + 31) // 32 * 32

    def sb(name, shape, dt, offset=None):
        if offset is None:
            n = 2 if dt == BF16 else 4
            for k in shape[1:]:
                n *= k
            n = (n + 31) // 32 * 32
            offset = at["small"]
            at["small"] += n
        return nc.alloc_sbuf_tensor_at(name, list(shape), dt, offset=base + offset)

    HT_H = sb("hT_high", [P, KC, S], F32R, 0)
    HT_L = sb("hT_low", [P, KC, S], F32R, 32768)
    RING = 4
    w_raw = sb("w_raw", [P, RING, BW], F32, 65536)
    w_high = sb("w_high", [P, RING, BW], F32R, 73728)
    w_low = sb("w_low", [P, RING, BW], F32R, 81920)
    NSA_AT, FM_AT, HV_AT = 90112, 131840, 164608
    nsa = sb("nsa", [P, NT, NSAW], F32, NSA_AT)
    fm = sb("hgrn_qf", [P, 2, NT, HH, P], F32, FM_AT)
    hv = sb("hgrn_vg", [P, 2, NT, HH * P], F32, HV_AT)
    x_in = sb("x_in", [P, NT, D], F32, NSA_AT)
    row = sb("normed_rows", [P, 2, D], F32, FM_AT)
    gain_row = sb("attn_gain", [P, D], F32, FM_AT + 8192)
    junk = sb("squares", [P, 2, D], F32, FM_AT + 12288)
    sq = sb("head_squares", [P, 2, NHEADCOL * DK], F32, HV_AT)
    rtmp = sb("rope_products", [P, 4, 14 * 8], F32, HV_AT + 9216)
    hsum, hrs_a, hrs_t, hrstd = (sb(n, [P, NT, 20], F32, HV_AT + 11264 + 640 * i)
                                 for i, n in enumerate(("h_sums", "h_rsqrt_a", "h_rsqrt_t", "h_rstd")))
    w1 = sb("cmp_w1", [P, 2, CMP_STEPS, P], F32, HV_AT)
    pairs = sb("cmp_tokens", [P, 2, NG, S // 2 + CMP_STEPS], F32, HV_AT + 16384)
    KS_H = sb("k_high", [P, 2, NG, S], F32R, 0)
    KS_L = sb("k_low", [P, 2, NG, S], F32R, 16384)
    QT = sb("q_stack", [P, 2, S], F32R, 32768)
    probs = sb("probs", [P, P_SLOTS, S], F32, 65536)
    pT = sb("probs_T", [P, PT_SLOTS, BW], F32, 40960)
    masks = sb("masks", [P, 3 * P], BF16, 61440)
    cmask = sb("cmask", [P, NT * NCP], BF16, 62464)
    cdiff = sb("cmp_diff", [P, BW], F32, 81920)
    stage = sb("stage", [P, 2, NT, 2, DK], F32)
    hk = sb("hgrn_k", [P, NT, BW], F32, 0)
    hlf = sb("hgrn_logf", [P, 4, 2 * BW], F32, 16384)
    hE = sb("hgrn_exp", [P, E_SLOTS, BW], F32, 16384)
    hK0 = sb("hgrn_k0", [P, BW], F32, 22528)
    hX = sb("hgrn_kq", [P, X_SLOTS, BW], F32, 24576)
    hD = sb("hgrn_diff", [P, D_SLOTS, BW], F32, 32768)
    tree = sb("tree_masks", [P, len(LEVELS) + 1, P], I32, 40960)
    hA = sb("hgrn_A", [P, BW], F32, 45056)
    hQe = sb("hgrn_qe", [P, BW], F32, 47104)
    hKd = sb("hgrn_kend", [P, BW], F32, 49152)
    hKT = sb("hgrn_kendT", [P, BW], F32, 51200)
    hst = sb("hgrn_state", [P, BW], F32, 53248)
    hDe = sb("hgrn_dend", [P, BW], F32, 55296)
    hEe = sb("hgrn_eend", [P, 2, BW], F32, 57344)
    hone = sb("hgrn_reset", [P, 2 * BW], F32, 61440)
    x1 = sb("x1", [P, NT, D], F32, FM_AT)
    row2 = sb("mixed_rows", [P, 2, D], F32, 197376)
    h1_H = sb("hidden_high", [P, 4, S], F32R, NSA_AT)
    h1_L = sb("hidden_low", [P, 4, S], F32R, NSA_AT + 16384)
    relu = sb("relu", [P, 4, BW], F32, HV_AT)
    relu2 = sb("relu_squared", [P, 4, BW], F32, HV_AT + 8192)
    junk2 = sb("squares2", [P, 2, D], F32, HV_AT + 16384)
    gain2 = sb("mlp_gain", [P, D], F32, HV_AT + 24576)
    rope = sb("rope", [P, NT, 16], F32)
    eye = sb("eye", [P, P], F32)
    qg = sb("q_gain", [P, DK], F32)
    kg = sb("k_gain", [P, DK], F32)
    gates = sb("gates", [P, NT, 24], F32)
    valid = sb("valid", [P, NT], F32)
    ssq, rs_a, rs_t, rstd = (sb(n, [P, 64], F32) for n in ("sums_of_squares", "rsqrt_a", "rsqrt_t", "rstd"))
    ssq2 = sb("sums_of_halves", [P, 2, NT], F32)
    eps = sb("eps", [P, 1], F32)
    unused = sb("unused", [P, 1], F32)
    pe_sb = sb("pe_rows", [CMP_STEPS, 2, P], F32, 197376)
    lb_rows = sb("lb_rows", [2 * HH, P], F32, 197376 + 1024)
    negmax = sb("negmax", [P, 34], F32, 63488)
    rsums = sb("row_sums", [P, 2, NT, 2], F32, 63648)
    coef = sb("coef", [P, 2, NT, 2], F32, 63776)
    cmx = sb("cmp_max", [P, 3, NT], F32, 63904)
    cbias = sb("cmp_bias", [P, 2], F32)
    lb = sb("lb", [P, 6, HH], F32)
    w2 = sb("cmp_w2", [P, 2, 2, DK], F32)
    kc = sb("cmp_k", [P, NG, NCP], F32)
    vc = sb("cmp_v", [P, 2, NG, DK], F32)
    assert base + at["small"] <= nc.sbuf_usable_end, (base, at["small"], nc.sbuf_usable_end)
    ps = nc.alloc_psum_tensor("ps", [P, 8, BW], F32)
    ps_bf = None

    def sem(name):
        return nc.alloc_semaphore(name)

    x_loaded = [sem(f"x_loaded{t}") for t in range(NT)]
    c_loaded = sem("constants_loaded")
    pool_set = sem("pool_set")
    w_loaded = [sem(f"w_loaded{i}") for i in range(RING)]
    w_highs = sem("w_highs")
    w_split = sem("w_split")
    w_used = sem("w_used")
    sums_ready = sem("sums_ready")
    logs_ready = sem("logs_ready")
    root_ready = sem("root_ready")
    norm_step = sem("norm_step")
    rows_ready = sem("rows_ready")
    rowsT_done = sem("rowsT_done")
    rows_high = sem("rows_high")
    rows_low = sem("rows_low")
    proj_full = sem("proj_full")
    proj_out = sem("proj_out")

    sq_ready = sem("head_squares_ready")
    sq_summed = sem("head_squares_summed")
    gates_done = sem("gates_done")
    prep_step = sem("prep_step")
    prep_done = sem("prep_done")
    c2_loaded = sem("cmp_w1_loaded")
    m_loaded = sem("masks_loaded")
    smallT = sem("pe_and_lb_transposed")
    smallT_out = sem("pe_and_lb_out")
    tokT_done = sem("cmp_tokens_transposed")
    tok_pairs = [sem("cmp_pairs_by_act"), sem("cmp_pairs_by_dve")]
    cb_ready = sem("cmp_bias_ready")
    hid_full = sem("cmp_hidden_full")
    hid_sig = sem("cmp_hidden_sigmoid")
    hid_step = sem("cmp_hidden_step")
    hid_ready = sem("cmp_hidden_ready")
    cmp_full = sem("cmp_full")
    cmp_out = sem("cmp_out")
    lb_exp = sem("lb_exp")

    stage_ready = sem("stage_ready")
    t_full = sem("t_full")
    t_act = sem("t_bank_emptied_by_act")
    t_dve = sem("t_bank_emptied_by_dve")
    qk_done = sem("qk_done")
    max_done = sem("max_done")
    exp_done = sem("exp_done")
    csum_done = sem("csum_done")
    pv_done = sem("pv_done")
    o_free = sem("o_free")
    att_step = sem("att_step")

    t_loaded = sem("tree_masks_loaded")
    fill_set = sem("hgrn_fill")
    ln_done = sem("hgrn_ln")
    k_done = sem("hgrn_one_minus_f")
    bc_done = sem("hgrn_sums")
    d_ready = sem("hgrn_d_ready")
    e_half = sem("hgrn_e_half")
    e_ready = sem("hgrn_e_ready")
    x_ready = sem("hgrn_kq_ready")
    k0_ready = sem("hgrn_k0_ready")
    A_full = sem("hgrn_A_full")
    A_merged = sem("hgrn_A_merged")
    eb_ready = sem("hgrn_exp_sums")
    de_ready = sem("hgrn_dend_ready")
    ee_ready = sem("hgrn_exp_end")
    qe_ready = sem("hgrn_qe_ready")
    kd_ready = sem("hgrn_kend_ready")
    KT_full = sem("hgrn_kendT_full")
    KT_ready = sem("hgrn_kendT_ready")
    st_full = sem("hgrn_outputs_full")
    ho_out = sem("hgrn_output_out")
    st_ready = sem("hgrn_state_ready")
    st_step = sem("hgrn_state_step")
    g_loaded = sem("mix_gains_loaded")
    g2_loaded = sem("mlp_gain_loaded")
    x2_loaded = sem("x_loaded_again")
    ysum_ready = sem("ysum_ready")
    mix_step = sem("mix_step")
    res_out = sem("residual_out")
    wo_full = sem("w_out_full")
    sum2_ready = sem("sum2_ready")
    m1_full = sem("hidden_full")
    m1_out = sem("hidden_out")
    sqd = sem("hidden_squared")
    h_high = sem("hidden_high_ready")
    h_low = sem("hidden_low_ready")
    m2_full = sem("mlp_out_full")
    out_sent = sem("out_sent")

    waits_passed = [sem("pool_waits_passed"), sem("dve_waits_passed")]

    NCONST = 12

    def stand_alone(eng):
        eng.sem_inc(waits_passed[eng is nc.vector])

    chunk_no = {"sp": 0, "pool": 0, "pe": 0}

    def load_chunk(eng, n, j, src, width=BW, first=False):
        if not first:
            eng.wait_ge(w_split, n + j - RING + 1)
        eng.dma_start(w_raw[:, j % RING, 0:width], src).then_inc(w_loaded[j % RING], 16)

    def split_chunk(eng, n, n4, j, width=BW, first=False):
        s = j % RING
        eng.wait_ge(w_loaded[s], (n4 + j // RING + 1) * 16)
        if not first:
            eng.wait_ge(w_used, n + j - RING + 1)
        stand_alone(eng)
        eng.tensor_copy(w_high[:, s, 0:width], w_raw[:, s, 0:width]).then_inc(w_highs, 1)
        eng.wait_ge(w_highs, n + j + 1)
        eng.tensor_tensor(w_low[:, s, 0:width], w_raw[:, s, 0:width],
                          w_high[:, s, 0:width].bitcast(F32), ALU.subtract).then_inc(w_split, 1)

    def three_passes(out_ap, a_hl, b_hl, first, last):
        ins = None
        for n, (i, j) in enumerate(((0, 0), (0, 1), (1, 0))):
            ins = nc.tensor.matmul(out_ap, a_hl[i], b_hl[j], start=first and n == 0, stop=last and n == 2)
        return ins

    def chunk_signals(ins, b, k, full):
        if b == 7:
            ins.then_inc(w_used, 1)
        elif k == KC - 1:
            ins.then_inc(full, 1)

    def rows_chunk(pe, n, j, width, full, bank_free=None):
        s, k = j % RING, j % KC
        pe.wait_ge(w_split, n + j + 1)
        for t in range(NT):
            if k == 0 and bank_free is not None:
                bank_free(t)
            a = [h[:, k, t * P:(t + 1) * P] for h in (HT_H, HT_L)]
            b = [w[:, s, 0:width] for w in (w_high, w_low)]
            chunk_signals(three_passes(ps[:, t, 0:width], a, b, k == 0, k == KC - 1), t, k, full)

    def cols_chunk(pe, n, j, full, bank_free=None):
        s, k = j % RING, j % KC
        pe.wait_ge(w_split, n + j + 1)
        for b in range(8):
            c, half = divmod(b, 2)
            if k == 0 and bank_free is not None:
                bank_free(b)
            a = [w[:, s, c * P:(c + 1) * P] for w in (w_high, w_low)]
            r = [h[:, k, half * BW:(half + 1) * BW] for h in (HT_H, HT_L)]
            chunk_signals(three_passes(ps[:, b, :], a, r, k == 0, k == KC - 1), b, k, full)

    def transpose_rows(pe, r, t, src):
        pe.wait_ge(rows_ready, NT * r + t + 1)
        for j in range(2):
            n = 2 * t + j
            if n >= 4:
                pe.wait_ge(rows_low, 16 * r + n - 3)
            for q in range(4):
                c = 4 * j + q
                ins = nc.tensor.transpose(ps[:, n % 4, q * P:(q + 1) * P], src[:, t % 2, c * P:(c + 1) * P], eye[:])
            ins.then_inc(rowsT_done, 1)

    def hT_slice(h, j, t):
        return h[:, 4 * j:4 * j + 4, t * P:(t + 1) * P]

    def bank4(b):
        return ps[:, b, :].rearrange("p (q c) -> p q c", q=4)

    def high_half(act, r, n, j, t):
        act.wait_ge(rowsT_done, 16 * r + n + 1)
        nc.scalar.activation(hT_slice(HT_H, j, t), bank4(n % 4), ACT.Copy).then_inc(rows_high, 1)

    def low_half(dve, r, n, j, t):
        dve.wait_ge(rows_high, 16 * r + n + 1)
        nc.vector.tensor_tensor(hT_slice(HT_L, j, t), bank4(n % 4), hT_slice(HT_H, j, t).bitcast(F32),
                                ALU.subtract).then_inc(rows_low, 1)

    def high_rows(act, r, t):
        for j in range(2):
            high_half(act, r, 2 * t + j, j, t)

    def low_rows(dve, r, t):
        for j in range(2):
            low_half(dve, r, 2 * t + j, j, t)

    roots = {"act": 0, "dve": 0}
    vnorm = Steps(norm_step)

    norm_bufs = (ssq, rs_a, rs_t, rstd)

    head_bufs = [b[:, :, 0:NHEADCOL] for b in (hsum, hrs_a, hrs_t, hrstd)]

    def cols_of(a, b):
        return [x[:, a:b] for x in norm_bufs]

    def table_for(act, func):
        act.activation(unused[:], eps[:], func)

    def root_act(act, bufs, width):
        sums, _, log, root = bufs
        n = roots["act"] = roots["act"] + 1
        act.activation(log, sums, ACT.Ln, bias=eps[:, 0:1], scale=1.0 / width).then_inc(logs_ready, 1)
        act.wait_ge(logs_ready, n)
        act.activation(root, log, ACT.Exp, scale=-0.5).then_inc(root_ready, 1)

    def root_dve(dve, bufs, width):
        n = roots["dve"] = roots["dve"] + 1
        dve.wait_ge(root_ready, n)
        sums, a, t, r = bufs
        vnorm.mark(dve.tensor_scalar(a, sums, 1.0 / width, EPS, ALU.mult, ALU.add))
        vnorm.mark(dve.tensor_tensor(t, r, r, ALU.mult))
        vnorm.wait(dve)
        vnorm.mark(dve.tensor_tensor(t, t, a, ALU.mult))
        vnorm.wait(dve)
        vnorm.mark(dve.tensor_scalar(t, t, -0.5, 1.5, ALU.mult, ALU.add))
        vnorm.wait(dve)
        vnorm.mark(dve.tensor_tensor(r, r, t, ALU.mult))
        vnorm.wait(dve)

    hid2 = nsa[:, 0, KC0:KC0 + 2 * P]
    hid_e = nsa[:, 1, KC0:KC0 + P].rearrange("p (g n) -> p g n", g=NG)[:, :, 0:NCMP]
    CW = NCMP + 2
    hid_all = [ps[:, 5 + kv, 0:NG * CW].rearrange("p (g n) -> p g n", g=NG) for kv in range(2)]
    hid_ps = [h[:, :, 0:NCMP] for h in hid_all]

    def pair_tokens(eng_copy, kv, b):
        for g in range(NG):
            for a in range(2):
                eng_copy(pairs[a * DK:(a + 1) * DK, kv, g, b * BW // 2:(b + 1) * BW // 2],
                         ps[g * DK:(g + 1) * DK, 1 + 2 * kv + b, a:BW:2]).then_inc(tok_pairs[b], 1)

    it = Items()

    def key_stack(tensor, m):
        return tensor[:, m // 4, (m // 2) % 2, (m % 2) * BW:(m % 2 + 1) * BW]

    def stack_half(pe, m, slot, half):
        for q in range(4):
            ins = nc.tensor.transpose(ps[:, T_BANK + m % 2, q * P:(q + 1) * P],
                                      stage[:, slot, 4 * half + q, :, :].rearrange("p a d -> p (a d)"), eye[:])
        ins.then_inc(t_full, 1)

    def scores_view(j):
        w = len(it.items[j][3]) * P
        b = it.banks[j]
        return ps[:, b[0], 0:w] if w <= BW else ps[:, b[0]:b[0] + 2, 0:w // 2]

    def pt_free(eng, m, ib):
        n = it.groups[m]["ptn"] - PT_SLOTS
        if n >= 0:
            old = [u for u in it.groups if u.get("ptn") == n][0]
            eng.wait_ge(pv_done, ib + (old["item"] + 1))

    def tree_halves(ap, b):
        v = ap.rearrange("p (n c) -> p n c", c=2 * b)
        return v[:, :, 0:b], v[:, :, b:2 * b]

    def per_head(ap):
        return ap.rearrange("p (h t) -> p h t", h=HH)

    ngain = nsa[:, 0, KC0:KC0 + BW]
    hgain = nsa[:, 0, KW0:KW0 + P]
    junk_mix = [nsa[:, 5 + i, KC0:KC0 + BW] for i in range(2)]

    w_in0 = w_in[0]
    blocks = [(2 * BW, TAIL), (0, BW), (BW, BW), (HQ0, BW), (HQ0 + BW, BW), (HI0, BW), (HI0 + BW, BW)]
    W_OUT_AT = 8 * len(blocks)
    MLP_AT = W_OUT_AT + 16

    with nc.Block() as block:

        @block.sync
        def _(sp):
            for t in range(NT):
                sp.dma_start(x_in[:, t, :], x[0, t * P:(t + 1) * P, :]).then_inc(x_loaded[t], 16)
            for j in range(KC):
                load_chunk(sp, 0, j, w_in0[j * P:(j + 1) * P, 2 * BW:NSAW], TAIL, first=j < RING)
            for pair, col0 in enumerate((0, HQ0, HI0)):
                if pair == 2:
                    sp.wait_ge(prep_done, 1)
                    for kv, w in enumerate((cmp_w1_k, cmp_w1_v)):
                        sp.dma_start(w1[:, kv, :, :], w[0].rearrange("(s p) h -> p s h", p=P)).then_inc(c2_loaded, 16)
                with sp.Fori(0, 2) as i:
                    n = (i + (1 + 2 * pair)) * KC
                    for j in range(KC):
                        load_chunk(sp, n, j, w_in0[j * P:(j + 1) * P, bass.ds(i * BW + col0, BW)])
            sp.wait_ge(w_used, 8 * len(blocks))
            sp.dma_start(masks[:], c_masks.bitcast(BF16)).then_inc(m_loaded, 16)
            sp.dma_start(cmask[:], c_cmask.bitcast(BF16)).then_inc(m_loaded, 16)
            sp.wait_ge(o_free, 72)
            sp.dma_start(tree[:, :, :].rearrange("p n t -> p (n t)"), c_tree).then_inc(t_loaded, 16)
            sp.dma_start(ngain, nsa_out_norm[0].partition_broadcast(P)).then_inc(g_loaded, 16)
            sp.dma_start(hgain, hgrn_out_norm[0].partition_broadcast(P)).then_inc(g_loaded, 16)
            for blk in range(2):
                for k in range(KC):
                    if blk == 0 and k == RING:
                        sp.wait_ge(st_ready, NT + 1)
                        for t in range(NT):
                            sp.dma_start(x1[:, t, :], x[0, t * P:(t + 1) * P, :]).then_inc(x2_loaded, 16)
                    load_chunk(sp, W_OUT_AT, blk * KC + k, w_out[0, k * P:(k + 1) * P, blk * BW:(blk + 1) * BW])
            sp.wait_ge(rows_ready, 2 * NT)
            sp.dma_start(gain2[:], mlp_norm[0].partition_broadcast(P)).then_inc(g2_loaded, 16)
            with sp.Fori(0, NF) as i:
                for j in range(KC):
                    load_chunk(sp, i * 16 + MLP_AT, j, w_mlp_in[0, j * P:(j + 1) * P, bass.ds(i * BW, BW)])
                for j in range(KC):
                    half, fc = divmod(j, 4)
                    load_chunk(sp, i * 16 + MLP_AT, KC + j,
                               w_mlp_out[0, bass.ds(i * BW + fc * P, P), half * BW:(half + 1) * BW])
            for t in range(NT):
                sp.wait_ge(res_out, 16 * (NF + 1) - NT + t + 1)
                sp.dma_start(out[0, t * P:(t + 1) * P, :], x1[:, t, :]).then_inc(out_sent, 16)
            sp.wait_ge(out_sent, 16 * NT)

        @block.gpsimd
        def _(pool):
            pool.memset(eps[:], EPS).then_inc(pool_set, 1)
            pool.memset(vc[:], 0.0).then_inc(pool_set, 1)
            pool.wait_ge(pool_set, 2)
            for j in range(KC):
                split_chunk(pool, 0, 0, j, TAIL, first=j < RING)
            for pair in range(3):
                with pool.Fori(0, 2) as i:
                    for j in range(KC):
                        split_chunk(pool, (i + (1 + 2 * pair)) * KC, (i + (1 + 2 * pair)) * 2, j)

            def stage_head(n, slot, src):
                pool.tensor_copy(stage[:, slot, :, :, :], src.unsqueeze(2).to_broadcast([P, NT, 2, DK])).then_inc(stage_ready, 1)

            pool.wait_ge(hid_full, 2)
            for n in range(4):
                if n >= 2:
                    pool.wait_ge(t_full, 2 * (n - 1))
                col = (KS0, KW0)[n // 2] + (n % 2) * DK
                stage_head(n, n % 2, nsa[:, :, col:col + DK])
            pool.wait_ge(t_full, 6)
            stage_head(4, 0, nsa[:, :, Q0:Q0 + DK])
            with pool.Fori(0, NG) as g:
                with pool.Fori(0, 2) as pr:
                    trip = g * 2 + pr
                    pool.wait_ge(t_full, trip * len(it.groups) + FIRST)
                    stand_alone(pool)
                    stage_head(None, 1, nsa[:, :, bass.ds(g * 256 + pr * 128 + DK, DK)])
                    stage_head(None, 0, nsa[:, :, bass.ds(g * 256 + pr * 128 + 2 * DK, DK)])
            pool.wait_ge(o_free, 72)
            pool.memset(hone[:], 1.0).then_inc(fill_set, 1)
            pool.wait_ge(fill_set, 1)
            pool.memset(hone[:].rearrange("p (n t) -> p n t", t=P)[:, :, 0:1], 0.0).then_inc(fill_set, 1)
            for n in range(4):
                f2 = fm[:, 1, 2 * n:2 * n + 2, :, :].rearrange("p c h t -> p (c h t)")
                pool.tensor_scalar(hk[:, 2 * n:2 * n + 2, :].rearrange("p c x -> p (c x)"), f2, -1.0, 1.0,
                                   ALU.mult, ALU.add).then_inc(k_done, 1)
            pool.wait_ge(bc_done, 4)
            with pool.Fori(0, NT) as c:
                bc = fm[:, 1, bass.ds(c, 1), :, :].rearrange("p a h t -> p (a h t)")
                k_c = hk[:, bass.ds(c, 1), :].rearrange("p a x -> p (a x)")

                for n, b in enumerate(LEVELS):
                    if n >= D_SLOTS:
                        pool.wait_ge(e_ready, c * 7 + (n - D_SLOTS + 1))
                        stand_alone(pool)
                    v = bc.rearrange("p (n c) -> p n c", c=2 * b)
                    pool.tensor_tensor(hD[:, n % D_SLOTS, :].rearrange("p (n c) -> p n c", c=2 * b), v,
                                       v[:, :, b - 1:b].to_broadcast([P, BW // (2 * b), 2 * b]), ALU.subtract)\
                        .then_inc(d_ready, 1)
                v = per_head(bc)
                pool.tensor_tensor(per_head(hDe[:]), v[:, :, P - 1:P].to_broadcast([P, HH, P]), v, ALU.subtract)\
                    .then_inc(de_ready, 1)
                pool.wait_ge(ee_ready, c + 1)
                stand_alone(pool)
                pool.tensor_tensor(hKd[:], k_c, hEe[:, 1, :], ALU.mult).then_inc(kd_ready, 1)
                pool.wait_ge(eb_ready, c + 1)
                stand_alone(pool)
                pool.tensor_tensor(hQe[:], fm[:, 0, bass.ds(c, 1), :, :].rearrange("p a h t -> p (a h t)"), hEe[:, 0, :],
                                   ALU.mult).then_inc(qe_ready, 1)
            for j in range(16):
                split_chunk(pool, W_OUT_AT, W_OUT_AT // RING, j)
            with pool.Fori(0, NF) as i:
                for j in range(16):
                    split_chunk(pool, i * 16 + MLP_AT, i * 4 + MLP_AT // RING, j)

        @block.scalar
        def _(act):
            for dst, src in ((rope[:, :, :], c_rope.rearrange("(t p) c -> p t c", p=P)), (eye[:], c_eye),
                             (valid[:], c_valid),
                             (gain_row[:], attn_norm[0].partition_broadcast(P)),
                             (qg[:], q_norm[0].partition_broadcast(P)), (kg[:], k_norm[0].partition_broadcast(P)),
                             (pe_sb[:, 0, :], cmp_pe_k[0].rearrange("(s a) d -> s (a d)", a=2)),
                             (pe_sb[:, 1, :], cmp_pe_v[0].rearrange("(s a) d -> s (a d)", a=2)),
                             (w2[:, 0, 0, :], cmp_w2_k[0]), (w2[:, 0, 1, :], cmp_w2_k[0]),
                             (w2[:, 1, 0, :], cmp_w2_v[0]), (lb_rows[:], hgrn_lb.rearrange("l (h d) -> (l h) d", d=P))):
                act.dma_start(dst, src).then_inc(c_loaded, 16)
            act.wait_ge(pool_set, 1)
            table_for(act, ACT.Ln)
            for g in range(2):
                for t in range(4 * g, 4 * g + 4):
                    act.wait_ge(x_loaded[t], 16)
                    act.activation(junk[:, t % 2, :], x_in[:, t, :], ACT.Square, accum_out=ssq[:, t:t + 1])\
                        .then_inc(sums_ready, 1)
                    act.wait_ge(sums_ready, t + 1)
                root_act(act, cols_of(4 * g, 4 * g + 4), D)
                if g:
                    for t in range(4):
                        high_rows(act, 0, t)
            for t in range(4, NT):
                high_rows(act, 0, t)

            def evacuate(b, blk, dst, func=ACT.Copy):
                if b < 7:
                    act.wait_ge(proj_full, blk * 7 + b + 1)
                else:
                    act.wait_ge(w_used, (blk + 1) * KC)
                act.activation(dst, ps[:, b, 0:dst.shape[-1]] if len(dst.shape) == 2 else
                               ps[:, b, :].rearrange("p (c t) -> p c t", t=P), func).then_inc(proj_out, 1)

            for t in range(NT):
                evacuate(t, 0, nsa[:, t, 2 * BW:NSAW])
            with act.Fori(0, 2) as i:
                for t in range(NT):
                    evacuate(t, i + 1, nsa[:, t, bass.ds(i * BW, BW)])
            for t in range(NT):
                if t >= 2:
                    act.wait_ge(sq_summed, t - 1)
                else:
                    act.wait_ge(proj_out, 24)
                act.activation(sq[:, t % 2, :], nsa[:, t, 0:NHEADCOL * DK], ACT.Square).then_inc(sq_ready, 1)
            act.activation(gates[:, :, :], nsa[:, :, GT0:NSAW], ACT.Sigmoid).then_inc(gates_done, 1)
            act.wait_ge(sq_summed, NT)
            root_act(act, head_bufs, DK)
            for i, func in enumerate((ACT.Silu, ACT.Sigmoid)):
                for b in range(8):
                    c, half = divmod(b, 2)
                    evacuate(b, i + 3, fm[:, i, 4 * half:4 * half + 4, c, :], func)
            act.wait_ge(smallT, 1)
            pe_rows = ps[:, 0, 0:2 * CMP_STEPS].rearrange("p (k s) -> p k s", k=2).unsqueeze(2).to_broadcast([P, 2, NG, CMP_STEPS])
            act.activation(pairs[:, :, :, S // 2:], pe_rows, ACT.Copy).then_inc(smallT_out, 1)
            act.activation(lb[:, 0:2, :].rearrange("p a h -> p (a h)"), ps[:, 0, 64:64 + 2 * HH], ACT.Copy).then_inc(smallT_out, 1)
            act.wait_ge(hid_step, 3)
            act.activation(lb[:, 2:4, :], lb[:, 2:4, :], ACT.Exp).then_inc(lb_exp, 1)
            for kv in range(2):
                act.wait_ge(tokT_done, 2 * kv + 1)
                pair_tokens(lambda o, i: act.activation(o, i, ACT.Copy), kv, 0)
            for kv in range(2):
                act.wait_ge(hid_full, kv + 1)
                act.activation(cbias[:, kv:kv + 1], hid_all[kv][:, 0, CW - 1:CW], ACT.Copy).then_inc(cb_ready, 1)
                act.wait_ge(cb_ready, kv + 1)
                if kv:
                    act.wait_ge(hid_ready, 1)
                act.activation(hid_e, hid_ps[kv], ACT.Sigmoid, bias=cbias[:, kv:kv + 1]).then_inc(hid_sig, 1)
                act.wait_ge(cmp_full, kv + 1)
                if kv == 0:
                    act.activation(kc[:, :, :].rearrange("p g n -> p (g n)"), ps[:, 0, 0:P], ACT.Copy).then_inc(cmp_out, 1)
            act.wait_ge(pool_set, 2)
            for a in range(2):
                act.activation(vc[a * DK:(a + 1) * DK, a, :, :].rearrange("p g d -> p (g d)"),
                               ps[a * DK:(a + 1) * DK, 7, 0:P], ACT.Copy).then_inc(cmp_out, 1)
            for i, func in enumerate((ACT.Copy, ACT.Silu)):
                for t in range(NT):
                    evacuate(t, i + 5, hv[:, i, t, :], func)

            for m in range(8):
                act.wait_ge(t_full, m + 1)
                act.activation(key_stack(KS_H, m), ps[:, T_BANK + m % 2, :], ACT.Copy).then_inc(t_act, 1)

            for half in range(2):
                act.wait_ge(t_full, 8 + half + 1)
                act.activation(QT[:, 0, half * BW:(half + 1) * BW], ps[:, T_BANK + half, :], ACT.Copy).then_inc(t_act, 1)

            def att_act(g, pr):
                i = g * 2 + pr
                tb, ab, ib = i * len(it.groups) + FIRST, i * it.n_act + FIRST, i * len(it.items)

                def prep(hh):
                    for half, m in enumerate(it.prep[hh]):
                        act.wait_ge(t_full, tb + (m + 1))
                        act.activation(QT[:, hh, half * BW:(half + 1) * BW], ps[:, T_BANK + m % 2, :], ACT.Copy).then_inc(t_act, 1)

                def exponentials(j):
                    kind, hh, t, tiles = it.items[j]
                    act.wait_ge(max_done, ib + (j + 1))
                    act.wait_ge(t_full, tb + (it.of[j - P_SLOTS][-1] + 1 if j >= P_SLOTS else 0))
                    if kind == "cmp":
                        act.activation(probs[:, j % P_SLOTS, 0:BW], cdiff[:], ACT.Exp).then_inc(exp_done, 1)
                        return
                    if j in (P_SLOTS, it.per_head + P_SLOTS):
                        act.wait_ge(csum_done, i * 2 + (hh + 1))
                    sv = scores_view(j)
                    w = len(tiles) * P
                    o = probs[:, j % P_SLOTS, 0:w]
                    if len(sv.shape) == 3:
                        o = o.rearrange("p (a b) -> p a b", a=2)
                    act.activation(o, sv, ACT.Exp, bias=negmax[:, j:j + 1],
                                   accum_out=rsums[:, hh, t, int(kind == "win"):int(kind == "win") + 1]).then_inc(exp_done, 1)

                table_for(act, ACT.Exp)
                exponentials(0)
                exponentials(1)
                for j in range(len(it.items)):
                    if j in (PREP_AT, NEXT_AT):
                        prep(int(j == PREP_AT))
                    for m in it.of[j]:
                        if it.groups[m]["act"]:
                            act.wait_ge(t_full, tb + (m + 1))
                            pt_free(act, m, ib)
                            n = it.groups[m]["n"] * P
                            act.activation(pT[:, it.groups[m]["pt"], 0:n], ps[:, T_BANK + m % 2, 0:n], ACT.Copy).then_inc(t_act, 1)
                    if j + 2 < len(it.items):
                        exponentials(j + 2)

            with act.Fori(0, NG) as g:
                with act.Fori(0, 2) as pr:
                    att_act(g, pr)

            act.wait_ge(o_free, 72)
            for n in range(4):
                f2 = fm[:, 1, 2 * n:2 * n + 2, :, :].rearrange("p c h t -> p (c h t)")
                act.activation(hlf[:, n, :], f2, ACT.Ln).then_inc(ln_done, 1)
            for t in range(NT):
                if t >= 2:
                    act.wait_ge(ysum_ready, t - 1)
                act.activation(junk_mix[t % 2], nsa[:, t, 0:BW], ACT.Square, accum_out=ssq[:, t:t + 1]).then_inc(ysum_ready, 1)
            act.wait_ge(ysum_ready, NT)
            root_act(act, cols_of(0, NT), BW)
            with act.Fori(0, NT) as c:
                bc = fm[:, 1, bass.ds(c, 1), :, :].rearrange("p a h t -> p (a h t)")
                for n, b in enumerate(LEVELS):
                    act.wait_ge(d_ready, c * 7 + (n + 1))
                    if n >= E_SLOTS:
                        act.wait_ge(x_ready, c * 14 + 2 * (n - E_SLOTS + 1))
                    (d1, d2), (e1, e2) = tree_halves(hD[:, n % D_SLOTS, :], b), tree_halves(hE[:, n % E_SLOTS, :], b)
                    act.activation(e2, d2, ACT.Exp).then_inc(e_half, 1)
                    act.activation(e1, d1, ACT.Exp, scale=-1.0).then_inc(e_ready, 1)
                act.wait_ge(st_ready, c + 1)
                act.activation(hK0[:], hk[:, bass.ds(c, 1), :].rearrange("p a x -> p (a x)"), ACT.Copy).then_inc(k0_ready, 1)
                act.wait_ge(de_ready, c + 1)
                act.activation(hEe[:, 1, :], hDe[:], ACT.Exp).then_inc(ee_ready, 1)
                act.activation(hEe[:, 0, :], bc, ACT.Exp).then_inc(eb_ready, 1)
                act.wait_ge(KT_full, c + 1)
                act.activation(hKT[:], ps[:, 3, :], ACT.Copy).then_inc(KT_ready, 1)
                act.wait_ge(st_full, c + 1)
                act.activation(hv[:, 0, bass.ds(c, 1), :].rearrange("p a x -> p (a x)"), ps[:, 2, :], ACT.Copy)\
                    .then_inc(ho_out, 1)

            act.wait_ge(st_ready, NT + 1)
            act.wait_ge(ho_out, NT)
            for g in range(2):
                table_for(act, ACT.Ln)
                for t in range(4 * g, 4 * g + 4):
                    for h in range(HH):
                        n = NT + HH * t + h
                        if n >= NT + 2:
                            act.wait_ge(ysum_ready, n - 1)
                        act.activation(junk_mix[n % 2][:, 0:P], hv[:, 0, t, h * P:(h + 1) * P], ACT.Square,
                                       accum_out=ssq[:, n:n + 1]).then_inc(ysum_ready, 1)
                act.wait_ge(ysum_ready, NT + 4 * HH * (g + 1))
                root_act(act, cols_of(NT + 4 * HH * g, NT + 4 * HH * (g + 1)), P)
                for n in range(4 * g, 4 * g + (4 if g == 0 else 12)):
                    high_half(act, 1, n, *divmod(n, NT))

            table_for(act, ACT.Ln)
            for half in range(2):
                for t in range(NT):
                    n = NT * half + t
                    act.wait_ge(res_out, n + 1)
                    if n >= 2:
                        act.wait_ge(sum2_ready, n - 1)
                    act.activation(junk2[:, t % 2, 0:BW], x1[:, t, half * BW:(half + 1) * BW], ACT.Square,
                                   accum_out=ssq2[:, half, t:t + 1]).then_inc(sum2_ready, 1)
            act.wait_ge(sums_ready, NT + 1)
            root_act(act, cols_of(48, 48 + NT), D)
            for t in range(NT):
                high_rows(act, 2, t)

            with act.Fori(0, NF) as i:
                def high(b):
                    act.wait_ge(sqd, i * 8 + (b + 1))
                    c, half = divmod(b, 2)
                    act.activation(h1_H[:, c, half * BW:(half + 1) * BW], relu2[:, b % 4, :], ACT.Copy).then_inc(h_high, 1)

                for b in range(8):
                    if b < 7:
                        act.wait_ge(m1_full, i * 7 + (b + 1))
                    else:
                        act.wait_ge(w_used, i * 16 + (MLP_AT + KC))
                    act.activation(relu[:, b % 4, :], ps[:, b, :], ACT.Relu).then_inc(m1_out, 1)
                    if b:
                        high(b - 1)
                high(7)

        @block.vector
        def _(dve):
            dve.wait_ge(c_loaded, 16 * NCONST)
            def rows(t):
                if t >= 2:
                    dve.wait_ge(rowsT_done, 2 * (t - 1))
                dve.scalar_tensor_tensor(row[:, t % 2, :], x_in[:, t, :], rstd[:, t:t + 1], gain_row[:],
                                         ALU.mult, ALU.mult).then_inc(rows_ready, 1)
            for g in range(2):
                root_dve(dve, cols_of(4 * g, 4 * g + 4), D)
                for t in range(4 * g, 4 * g + 4):
                    rows(t)
                    if t:
                        low_rows(dve, 0, t - 1)
            low_rows(dve, 0, NT - 1)

            for t in range(NT):
                dve.wait_ge(sq_ready, t + 1)
                dve.tensor_reduce(hsum[:, t, 0:NHEADCOL],
                                  sq[:, t % 2, :].rearrange("p (h d) -> p h d", d=DK), AX, ALU.add).then_inc(sq_summed, 1)
            st = Steps(prep_step)
            st.mark(dve.tensor_scalar(qg[:], qg[:], DK ** -0.5, None, ALU.mult))
            dve.wait_ge(gates_done, 1)
            g0 = gates[:, :, :].rearrange("p t (h b) -> p t h b", b=3)[:, :, :, 0]
            st.mark(dve.tensor_tensor(g0, g0, valid[:].unsqueeze(2).to_broadcast([P, NT, NH]), ALU.mult))
            root_dve(dve, head_bufs, DK)
            with dve.Fori(0, NT) as t:
                st.enter(t, 16)
                qv = nsa[:, bass.ds(t, 1), 0:KC0].rearrange("p a (h d) -> p (a h) d", d=DK)
                kv = nsa[:, bass.ds(t, 1), KC0:GT0].rearrange("p a (b c) -> p (a b) c", b=3)[:, :, 0:NG * DK]\
                    .rearrange("p b (g d) -> p b g d", d=DK)
                qr = hrstd[:, bass.ds(t, 1), 0:NH].rearrange("p a h -> p (a h)").unsqueeze(2).to_broadcast([P, NH, DK])
                kr = hrstd[:, bass.ds(t, 1), NH:20].rearrange("p a (b c) -> p (a b) c", c=4)[:, :, 0:NG]\
                    .unsqueeze(3).to_broadcast([P, 3, NG, DK])
                st.mark(dve.tensor_tensor(qv, qv, qr, ALU.mult))
                st.mark(dve.tensor_tensor(kv, kv, kr, ALU.mult))
                st.wait(dve)
                st.mark(dve.tensor_tensor(qv, qv, qg[:].unsqueeze(1).to_broadcast([P, NH, DK]), ALU.mult))
                st.mark(dve.tensor_tensor(kv, kv, kg[:].unsqueeze(1).unsqueeze(1).to_broadcast([P, 3, NG, DK]), ALU.mult))
                st.wait(dve)
                for part in range(2):
                    if part == 0:
                        ra, rb = qv[:, :, 0:8], qv[:, :, 8:16]
                        co, si = (rope[:, bass.ds(t, 1), 8 * i:8 * i + 8].to_broadcast([P, NH, 8]) for i in range(2))
                        tm = [rtmp[:, i, 0:64].rearrange("p (h e) -> p h e", e=8) for i in range(4)]
                    else:
                        ra, rb = kv[:, :, :, 0:8], kv[:, :, :, 8:16]
                        co, si = (rope[:, bass.ds(t, 1), 8 * i:8 * i + 8].unsqueeze(1).to_broadcast([P, 3, NG, 8]) for i in range(2))
                        tm = [rtmp[:, i, 64:112].rearrange("p (b g e) -> p b g e", g=NG, e=8) for i in range(4)]
                    for i, (u, v_) in enumerate(((ra, co), (rb, si), (rb, co), (ra, si))):
                        st.mark(dve.tensor_tensor(tm[i], u, v_, ALU.mult))
                    st.wait(dve)
                    st.mark(dve.tensor_tensor(ra, tm[0], tm[1], ALU.subtract))
                    st.mark(dve.tensor_tensor(rb, tm[2], tm[3], ALU.add))
                st.wait(dve)
            st.leave(NT)
            dve.tensor_copy(qg[:, 0:1], qg[:, 0:1]).then_inc(prep_done, 1)

            hs = Steps(hid_step)
            dve.wait_ge(smallT_out, 2)
            hs.mark(dve.tensor_tensor(lb[:, 4, :], lb[:, 0, :], lb[:, 1, :], ALU.max))
            hs.wait(dve)
            hs.mark(dve.tensor_tensor(lb[:, 2, :], lb[:, 0, :], lb[:, 4, :], ALU.subtract))
            hs.mark(dve.tensor_tensor(lb[:, 3, :], lb[:, 1, :], lb[:, 4, :], ALU.subtract))
            dve.wait_ge(lb_exp, 1)
            hs.mark(dve.tensor_tensor(lb[:, 4, :], lb[:, 2, :], lb[:, 3, :], ALU.add))
            hs.wait(dve)
            hs.mark(dve.reciprocal(lb[:, 4, :], lb[:, 4, :]))
            hs.wait(dve)
            hs.mark(dve.tensor_tensor(lb[:, 0, :], lb[:, 2, :], lb[:, 4, :], ALU.mult))
            hs.wait(dve)
            hs.mark(dve.tensor_scalar(lb[:, 1, :], lb[:, 0, :], -1.0, 1.0, ALU.mult, ALU.add))
            for kv in range(2):
                dve.wait_ge(tokT_done, 2 * kv + 2)
                pair_tokens(dve.tensor_copy, kv, 1)
            hs.mark(dve.memset(hid2, 0.0))
            for kv in range(2):
                dve.wait_ge(hid_sig, kv + 1)
                hs.wait(dve)
                if kv:
                    dve.wait_ge(cmp_full, 1)
                for a in range(2):
                    ins = dve.scalar_tensor_tensor(hid2.rearrange("p (g a n) -> p g a n", g=NG, a=2)[:, :, a, 0:NCMP],
                                                   hid_ps[kv], cbias[:, kv:kv + 1], hid_e, ALU.add, ALU.mult)
                    ins.then_inc(hid_ready, 1) if a else hs.mark(ins)

            dve.wait_ge(proj_out, 40)
            for h in range(HH):
                dve.tensor_scalar(fm[:, 1, :, h, :], fm[:, 1, :, h, :], lb[:, 1, h:h + 1], lb[:, 0, h:h + 1], ALU.mult, ALU.add)

            for m in range(8):
                dve.wait_ge(t_act, m + 1)
                dve.tensor_tensor(key_stack(KS_L, m), ps[:, T_BANK + m % 2, :], key_stack(KS_H, m).bitcast(F32),
                                  ALU.subtract).then_inc(t_dve, 1)
            for half in range(2):
                dve.wait_ge(t_act, 8 + half + 1)
                q = QT[DK:P, 0, half * BW:(half + 1) * BW]
                dve.tensor_tensor(q, ps[DK:P, T_BANK + half, :], q.bitcast(F32), ALU.subtract).then_inc(t_dve, 1)
            at_ = Steps(att_step)

            def att_dve(g, pr):
                i = g * 2 + pr
                tb, ab, vb, ib = i * len(it.groups) + FIRST, i * it.n_act + FIRST, i * it.n_dve + FIRST, i * len(it.items)

                def prep(hh):
                    for half, m in enumerate(it.prep[hh]):
                        dve.wait_ge(t_act, ab + it.groups[m]["act_after"])
                        q = QT[DK:P, hh, half * BW:(half + 1) * BW]
                        dve.tensor_tensor(q, ps[DK:P, T_BANK + m % 2, :], q.bitcast(F32), ALU.subtract).then_inc(t_dve, 1)

                def maximum(j):
                    kind, hh, t, tiles = it.items[j]
                    dve.wait_ge(qk_done, ib + (j + 1))
                    if kind != "cmp":
                        sv = scores_view(j)
                        dve.tensor_reduce(negmax[:, j:j + 1], sv, AX if len(sv.shape) == 2 else mybir.AxisListType.XY,
                                          ALU.max, negate=True).then_inc(max_done, 1)
                        return
                    sv = ps[:, it.banks[j][0], :].rearrange("p (t n) -> p t n", n=NCP)
                    at_.mark(dve.tensor_reduce(cmx[:, 0, :], sv, AX, ALU.max))
                    at_.wait(dve)
                    dve.tensor_tensor(cdiff[:].rearrange("p (t n) -> p t n", n=NCP), sv,
                                      cmx[:, 0, :].unsqueeze(2).to_broadcast([P, NT, NCP]), ALU.subtract).then_inc(max_done, 1)

                def finalize(j):
                    kind, hh, t, tiles = it.items[j]
                    head3 = g * 12 + pr * 6 + 3 * hh
                    ycol = g * 256 + pr * 128 + hh * DK
                    if kind == "slc":
                        return
                    if kind == "cmp":
                        y = nsa[:, :, bass.ds(ycol, DK)]
                        at_.mark(dve.reciprocal(cmx[:, 2, :], cmx[:, 1, :]))
                        at_.wait(dve)
                        at_.mark(dve.tensor_tensor(cmx[:, 2, :], cmx[:, 2, :],
                                                   gates[:, :, bass.ds(head3, 1)].rearrange("p t a -> p (t a)"), ALU.mult))
                        at_.wait(dve)
                        dve.wait_ge(pv_done, ib + (j + 1))
                        dve.tensor_tensor(y, ps[:, it.banks[j][0], :].rearrange("p (t d) -> p t d", d=DK),
                                          cmx[:, 2, :].unsqueeze(2).to_broadcast([P, NT, DK]), ALU.mult).then_inc(o_free, 1)
                        return
                    y = nsa[:, t, bass.ds(ycol, DK)]
                    c = coef[:, hh, t, :]
                    dve.wait_ge(exp_done, ib + (j + 1))
                    at_.mark(dve.reciprocal(c, rsums[:, hh, t, :]))
                    at_.wait(dve)
                    at_.mark(dve.tensor_tensor(c, c, gates[:, t, bass.ds(head3 + 1, 2)], ALU.mult))
                    at_.wait(dve)
                    dve.wait_ge(pv_done, ib + (j + 1))
                    dve.wait_ge(o_free, i * 18 + (hh * 9 + 1))
                    o_bank = O_BANK + it.pair(j) % 2
                    at_.mark(dve.scalar_tensor_tensor(y, ps[:, o_bank, 0:DK], coef[:, hh, t, 0:1], y, ALU.mult, ALU.add))
                    at_.wait(dve)
                    dve.scalar_tensor_tensor(y, ps[:, o_bank, DK:2 * DK], coef[:, hh, t, 1:2], y, ALU.mult, ALU.add)\
                        .then_inc(o_free, 1)

                maximum(0)
                maximum(1)
                for j in range(len(it.items)):
                    if j in (PREP_AT, NEXT_AT):
                        prep(int(j == PREP_AT))
                    if j + 2 < len(it.items):
                        maximum(j + 2)
                    kind, hh, t, tiles = it.items[j]
                    if kind == "cmp":
                        dve.wait_ge(exp_done, ib + (j + 1))
                        dve.tensor_reduce(cmx[:, 1, :], probs[:, j % P_SLOTS, 0:BW].rearrange("p (t n) -> p t n", n=NCP),
                                          AX, ALU.add).then_inc(csum_done, 1)
                    for m in it.of[j]:
                        if it.groups[m]["dve"]:
                            dve.wait_ge(t_full, tb + (m + 1))
                            pt_free(dve, m, ib)
                            n = it.groups[m]["n"] * P
                            dve.tensor_copy(pT[:, it.groups[m]["pt"], 0:n], ps[:, T_BANK + m % 2, 0:n]).then_inc(t_dve, 1)
                    if j >= 2:
                        if it.items[j - 2][0] == "cmp":
                            dve.wait_ge(csum_done, i * 2 + (it.items[j - 2][1] + 1))
                        finalize(j - 2)
                finalize(len(it.items) - 1)

            with dve.Fori(0, NG) as g:
                with dve.Fori(0, 2) as pr:
                    at_.enter(g * 2 + pr, 2 * (3 + 3 * NT))
                    att_dve(g, pr)
            at_.leave(4)

            dve.wait_ge(fill_set, 2)
            dve.wait_ge(t_full, FIRST + 4 * len(it.groups))
            dve.memset(hA[:], 0.0)
            dve.memset(hst[:], 0.0).then_inc(st_ready, 1)
            for n in range(4):
                f2 = fm[:, 1, 2 * n:2 * n + 2, :, :].rearrange("p c h t -> p (c h t)")
                dve.wait_ge(ln_done, n + 1)
                dve.wait_ge(k_done, n + 1)
                dve.tensor_tensor_scan(f2, hone[:], hlf[:, n, :], 0.0, ALU.mult, ALU.add).then_inc(bc_done, 1)
            dve.wait_ge(bc_done, 4)
            dve.wait_ge(t_loaded, 16)
            root_dve(dve, cols_of(0, NT), BW)
            dve.wait_ge(g_loaded, 32)
            sst, mx = Steps(st_step), Steps(mix_step)
            with dve.Fori(0, NT) as c:
                sst.enter(c, HH - 1)
                mx.enter(c, 2)
                q_c = fm[:, 0, bass.ds(c, 1), :, :].rearrange("p a h t -> p (a h t)")
                k_c = hk[:, bass.ds(c, 1), :].rearrange("p a x -> p (a x)")

                def merge(u):
                    dve.wait_ge(A_full, c * 8 + (u + 1))
                    if u:
                        dve.wait_ge(A_merged, c * 8 + u)
                    stand_alone(dve)
                    dve.copy_predicated(per_head(hA[:]), tree[:, u, :].unsqueeze(1).to_broadcast([P, HH, P]),
                                        per_head(ps[:, A_BANKS[u % len(A_BANKS)], :])).then_inc(A_merged, 1)

                for n, b in enumerate(LEVELS):
                    dve.wait_ge(e_half, c * 7 + (n + 1))
                    if n >= X_SLOTS:
                        dve.wait_ge(A_full, c * 8 + (n - X_SLOTS + 1))
                    x_, e_ = tree_halves(hX[:, n % X_SLOTS, :], b), tree_halves(hE[:, n % E_SLOTS, :], b)
                    dve.tensor_tensor(x_[1], tree_halves(q_c, b)[1], e_[1], ALU.mult).then_inc(x_ready, 1)
                    dve.wait_ge(e_ready, c * 7 + (n + 1))
                    dve.tensor_tensor(x_[0], tree_halves(k_c, b)[0], e_[0], ALU.mult).then_inc(x_ready, 1)
                    if n >= 2:
                        merge(n - 2)
                for u in range(5, 8):
                    merge(u)
                gt = hv[:, 1, bass.ds(c, 1), :].rearrange("p a x -> p (a x)")
                mx.mark(dve.tensor_tensor(per_head(gt), per_head(gt), hgain.unsqueeze(1).to_broadcast([P, HH, P]), ALU.mult))
                y = nsa[:, bass.ds(c, 1), 0:BW].rearrange("p a x -> p (a x)")
                mx.mark(dve.scalar_tensor_tensor(y, y, rstd[:, bass.ds(c, 1)], ngain, ALU.mult, ALU.mult))
                dve.wait_ge(st_full, c + 1)
                for h in range(HH):
                    cols = slice(h * P, (h + 1) * P)
                    ins = dve.scalar_tensor_tensor(hst[:, cols], hst[:, cols], hEe[:, 0, (h + 1) * P - 1:(h + 1) * P],
                                                   ps[:, 4, cols], ALU.mult, ALU.add)
                    ins.then_inc(st_ready, 1) if h == HH - 1 else sst.mark(ins)
            sst.leave(NT)
            mx.leave(NT)

            mx.wait(dve)
            for g in range(2):
                root_dve(dve, cols_of(NT + 4 * HH * g, NT + 4 * HH * (g + 1)), P)
                for t in range(4 * g, 4 * g + 4):
                    o = hv[:, 0, t, :]
                    mx.mark(dve.tensor_tensor(per_head(o), per_head(o), rstd[:, NT + HH * t:NT + HH * (t + 1)].unsqueeze(2)
                                              .to_broadcast([P, HH, P]), ALU.mult))
                    low_half(dve, 1, t, 0, t)
                    mx.wait(dve)
                    dve.tensor_tensor(o, o, hv[:, 1, t, :], ALU.mult).then_inc(rows_ready, 1)
            for t in range(NT):
                low_half(dve, 1, NT + t, 1, t)

            def add_banks(full, count, used, half):
                for t in range(NT):
                    if t < 7:
                        dve.wait_ge(full, count + (t + 1))
                    else:
                        dve.wait_ge(w_used, used)
                    xs = x1[:, t, half * BW:(half + 1) * BW]
                    dve.tensor_tensor(xs, ps[:, t, :], xs, ALU.add).then_inc(res_out, 1)

            dve.wait_ge(x2_loaded, 16 * NT)
            for half in range(2):
                add_banks(wo_full, 7 * half, W_OUT_AT + KC * (half + 1), half)

            dve.wait_ge(g2_loaded, 16)
            dve.wait_ge(sum2_ready, 2 * NT)
            dve.tensor_tensor(ssq[:, 48:48 + NT], ssq2[:, 0, :], ssq2[:, 1, :], ALU.add).then_inc(sums_ready, 1)
            root_dve(dve, cols_of(48, 48 + NT), D)
            for t in range(NT):
                if t < 2:
                    dve.wait_ge(rowsT_done, 32)
                else:
                    dve.wait_ge(rowsT_done, 32 + 2 * (t - 1))
                dve.scalar_tensor_tensor(row2[:, t % 2, :], x1[:, t, :], rstd[:, 48 + t:49 + t], gain2[:],
                                         ALU.mult, ALU.mult).then_inc(rows_ready, 1)
                if t:
                    low_rows(dve, 2, t - 1)
            low_rows(dve, 2, NT - 1)

            with dve.Fori(0, NF) as i:
                def low(b):
                    dve.wait_ge(h_high, i * 8 + (b + 1))
                    c, half = divmod(b, 2)
                    cols = slice(half * BW, (half + 1) * BW)
                    dve.tensor_tensor(h1_L[:, c, cols], relu2[:, b % 4, :], h1_H[:, c, cols].bitcast(F32), ALU.subtract)\
                        .then_inc(h_low, 1)

                for b in range(8):
                    dve.wait_ge(m1_out, i * 8 + (b + 1))
                    dve.tensor_tensor(relu2[:, b % 4, :], relu[:, b % 4, :], relu[:, b % 4, :], ALU.mult).then_inc(sqd, 1)
                    if b:
                        low(b - 1)
                low(7)
                for half in range(2):
                    add_banks(m2_full, i * 14 + 7 * half, i * 16 + (MLP_AT + KC + 4 * (half + 1)), half)

        @block.tensor
        def _(pe):
            pe.wait_ge(c_loaded, 16 * NCONST)
            for t in range(NT):
                transpose_rows(pe, 0, t, row)

            def compress_pe(pe):
                pe.wait_ge(proj_out, 40)
                for kv in range(2):
                    nc.tensor.transpose(ps[:, 0, kv * CMP_STEPS:(kv + 1) * CMP_STEPS], pe_sb[:, kv, :],
                                        eye[0:CMP_STEPS, 0:CMP_STEPS])
                nc.tensor.transpose(ps[:, 0, 64:64 + 2 * HH], lb_rows[:], eye[0:2 * HH, 0:2 * HH]).then_inc(smallT, 1)
                pe.wait_ge(prep_done, 1)
                for kv in range(2):
                    for t in range(NT):
                        ins = nc.tensor.transpose(ps[:, 1 + 2 * kv + t // 4, (t % 4) * P:(t % 4 + 1) * P],
                                                  nsa[:, t, KC0 + kv * P:KC0 + (kv + 1) * P], eye[:])
                        if t % 4 == 3:
                            ins.then_inc(tokT_done, 1)
                pe.wait_ge(c2_loaded, 32)
                pe.wait_ge(smallT_out, 1)
                for kv in range(2):
                    for b in range(2):
                        pe.wait_ge(tok_pairs[b], 4 * (kv + 1))
                    for n in range(CMP_STEPS):
                        ins = nc.tensor.matmul(hid_all[kv], w1[:, kv, n, :], pairs[:, kv, :, n:n + 8 * (CW - 1) + 1:8],
                                               start=n == 0, stop=n == CMP_STEPS - 1)
                    ins.then_inc(hid_full, 1)
                for kv in range(2):
                    pe.wait_ge(hid_ready, kv + 1)
                    h2 = hid2.rearrange("p (g a n) -> p g a n", g=NG, a=2)
                    if kv == 0:
                        nc.tensor.matmul(ps[:, 0, 0:P].rearrange("p (g n) -> p g n", g=NG), w2[:, 0, :, :].rearrange("p a d -> p (a d)"),
                                         h2[:, :, 0, :], start=True, stop=True).then_inc(cmp_full, 1)
                    else:
                        for g in range(NG):
                            ins = nc.tensor.matmul(ps[:, 7, g * DK:(g + 1) * DK], h2[:, g, :, :].rearrange("p a n -> p (a n)"),
                                                   w2[:, 1, 0, :], start=True, stop=True)
                        ins.then_inc(cmp_full, 1)
                pe.wait_ge(cmp_out, 3)

            pe.wait_ge(rows_low, 2 * NT)
            for j in range(KC):
                rows_chunk(pe, 0, j, TAIL, proj_full)

            def freed(blk):
                return lambda b: pe.wait_ge(proj_out, (blk - 1) * 8 + (b + 1))

            for pair in range(3):
                if pair == 2:
                    compress_pe(pe)
                with pe.Fori(0, 2) as i:
                    blk = i + (1 + 2 * pair)
                    for j in range(KC):
                        if pair == 1:
                            cols_chunk(pe, blk * KC, j, proj_full, freed(blk))
                        else:
                            rows_chunk(pe, blk * KC, j, BW, proj_full, freed(blk))

            pe.wait_ge(proj_out, 8 * len(blocks))
            for m in range(8):
                n, half = divmod(m, 2)
                if half == 0:
                    pe.wait_ge(stage_ready, n + 1)
                if m >= 2:
                    pe.wait_ge(t_dve, m - 1)
                stack_half(pe, m, n % 2, half)
            pe.wait_ge(stage_ready, 5)
            for half in range(2):
                pe.wait_ge(t_dve, 7 + half)
                stack_half(pe, 8 + half, 0, half)
            pe.wait_ge(m_loaded, 32)

            def att_pe(g, pr):
                i = g * 2 + pr
                ab, vb, ib = i * it.n_act + FIRST, i * it.n_dve + FIRST, i * len(it.items)

                def bank_free(m):
                    if m < 2:
                        pe.wait_ge(t_act, ab)
                        pe.wait_ge(t_dve, vb)
                        return
                    u = it.groups[m - 2]
                    if u["act"]:
                        pe.wait_ge(t_act, ab + u["act_after"])
                    if u["dve"]:
                        pe.wait_ge(t_dve, vb + u["dve_after"])

                def prep(hh):
                    pe.wait_ge(stage_ready, i * 2 + (7 - hh))
                    for half, m in enumerate(it.prep[hh]):
                        bank_free(m)
                        stack_half(pe, m, hh, half)

                def scores(j):
                    kind, hh, t, tiles = it.items[j]
                    banks = it.banks[j]
                    s_ = banks[0]
                    for u in it.before[j]:
                        if u > j - AHEAD:
                            pe.wait_ge(exp_done, ib + (u + 1))
                        if it.items[u][0] == "cmp":
                            pe.wait_ge(o_free, i * 18 + (it.items[u][1] * 9 + 1))
                    if kind == "cmp":
                        pe.wait_ge(t_dve, vb + (it.groups[it.prep[1][1]]["dve_after"] if hh else 0))
                        nc.tensor.matmul(ps[:, s_, :], masks[:, 0:P], cmask[:], start=True, stop=False, skip_group_check=True)
                        for t in range(NT):
                            o = ps[:, s_, t * NCP:(t + 1) * NCP]
                            ins = nc.tensor.matmul(o, QT[:, hh, t * P:(t + 1) * P].bitcast(F32),
                                                   kc[:, bass.ds(g, 1), :].rearrange("p a n -> p (a n)"),
                                                   start=False, stop=t == NT - 1, skip_group_check=True)
                        ins.then_inc(qk_done, 1)
                        return
                    br = int(kind == "win")
                    w = max(2, len(tiles)) * P
                    nb = 1 if w <= BW else 2
                    mask_at = {(nb - 1, len(tiles) * P // nb - P): 1}
                    if br and t >= WIN_T:
                        mask_at[(0, 0)] = 2
                    ms = [(b, c, k) for (b, c), k in mask_at.items()]
                    for b in range(nb):
                        o = ps[:, banks[b], 0:w // nb]
                        mine = [(c, k) for bb, c, k in ms if bb == b]
                        for n, k_ in enumerate((KS_H, KS_L)):
                            ins = nc.tensor.matmul(o, QT[:, hh, t * P:(t + 1) * P],
                                                   k_[:, br, bass.ds(g, 1), tiles[0] * P + b * (w // nb):tiles[0] * P + (b + 1) * (w // nb)]
                                                   .rearrange("p a n -> p (a n)"),
                                                   start=n == 0, stop=n == 1 and not mine, skip_group_check=True)
                        for q, (c, k) in enumerate(mine):
                            ins = nc.tensor.matmul(ps[:, banks[b], c:c + P], masks[:, 0:P], masks[:, k * P:(k + 1) * P],
                                                   start=False, stop=q == len(mine) - 1, skip_group_check=True)
                    ins.then_inc(qk_done, 1)

                def transposes(j):
                    pe.wait_ge(exp_done, ib + (j + 1))
                    for m in it.of[j]:
                        bank_free(m)
                        u = it.groups[m]
                        for q in range(u["n"]):
                            ins = nc.tensor.transpose(ps[:, T_BANK + m % 2, q * P:(q + 1) * P],
                                                      probs[:, j % P_SLOTS, (u["first"] + q) * P:(u["first"] + q + 1) * P], eye[:])
                        ins.then_inc(t_full, 1)

                def outputs(j):
                    kind, hh, t, tiles = it.items[j]
                    if kind == "slc" and it.pair(j) >= 2:
                        pe.wait_ge(o_free, i * 18 + it.pair_end(it.pair(j) - 2))
                    for m in it.of[j]:
                        u = it.groups[m]
                        if u["act"]:
                            pe.wait_ge(t_act, ab + u["act_after"])
                        else:
                            pe.wait_ge(t_dve, vb + u["dve_after"])
                        for q in range(u["n"]):
                            lhs = pT[:, u["pt"], q * P:(q + 1) * P]
                            if kind == "cmp":
                                for half in range(2):
                                    t2 = 2 * q + half
                                    ins = nc.tensor.matmul(ps[:, it.banks[j][0], t2 * DK:(t2 + 1) * DK], lhs,
                                                           vc[:, half, bass.ds(g, 1), :].rearrange("p a d -> p (a d)"),
                                                           start=True, stop=True)
                            else:
                                n = u["first"] + q
                                c, v0 = (DK, VW0) if kind == "win" else (0, VS0)
                                ins = nc.tensor.matmul(ps[:, O_BANK + it.pair(j) % 2, c:c + DK], lhs, nsa[:, tiles[n], bass.ds(g * DK + v0, DK)],
                                                       start=n == 0, stop=n == len(tiles) - 1)
                    ins.then_inc(pv_done, 1)

                for j in range(AHEAD):
                    scores(j)
                for j in range(len(it.items)):
                    if j in (PREP_AT, NEXT_AT):
                        prep(int(j == PREP_AT))
                    transposes(j)
                    if j + AHEAD < len(it.items):
                        scores(j + AHEAD)
                    if j:
                        outputs(j - 1)
                outputs(len(it.items) - 1)

            with pe.Fori(0, NG) as g:
                with pe.Fori(0, 2) as pr:
                    att_pe(g, pr)

            pe.wait_ge(bc_done, 4)
            with pe.Fori(0, NT) as c:
                def product(u, lhs, rhs):
                    for h in range(HH):
                        ins = nc.tensor.matmul(ps[:, A_BANKS[u % len(A_BANKS)], h * P:(h + 1) * P], lhs(h), rhs(h),
                                               start=True, stop=True)
                    ins.then_inc(A_full, 1)

                for n in range(len(LEVELS)):
                    pe.wait_ge(x_ready, c * 14 + 2 * (n + 1))
                    if n >= len(A_BANKS):
                        pe.wait_ge(A_merged, c * 8 + (n - len(A_BANKS) + 1))
                    x_ = [hX[:, n % X_SLOTS, h * P:(h + 1) * P] for h in range(HH)]
                    product(n, lambda h: x_[h], lambda h: x_[h])
                pe.wait_ge(k0_ready, c + 1)
                pe.wait_ge(A_merged, c * 8 + (8 - len(A_BANKS)))
                product(7, lambda h: hK0[:, h * P:(h + 1) * P],
                        lambda h: fm[:, 0, bass.ds(c, 1), h, :].rearrange("p a t -> p (a t)"))
                pe.wait_ge(kd_ready, c + 1)
                for h in range(HH):
                    ins = nc.tensor.transpose(ps[:, 3, h * P:(h + 1) * P], hKd[:, h * P:(h + 1) * P], eye[:])
                ins.then_inc(KT_full, 1)
                pe.wait_ge(KT_ready, c + 1)
                pe.wait_ge(qe_ready, c + 1)
                pe.wait_ge(A_merged, c * 8 + 8)
                pe.wait_ge(st_ready, c + 1)
                v = [hv[:, 0, bass.ds(c, 1), h * P:(h + 1) * P].rearrange("p a x -> p (a x)") for h in range(HH)]
                for h in range(HH):
                    cols = slice(h * P, (h + 1) * P)
                    nc.tensor.matmul(ps[:, 2, cols], hA[:, cols], v[h], start=True, stop=False)
                    nc.tensor.matmul(ps[:, 2, cols], hQe[:, cols], hst[:, cols], start=False, stop=True)
                for h in range(HH):
                    cols = slice(h * P, (h + 1) * P)
                    ins = nc.tensor.matmul(ps[:, 4, cols], hKT[:, cols], v[h], start=True, stop=True)
                ins.then_inc(st_full, 1)

            pe.wait_ge(st_ready, NT + 1)
            pe.wait_ge(ho_out, NT)
            for n in range(2 * NT):
                j, t = divmod(n, NT)
                if j:
                    pe.wait_ge(rows_ready, NT + t + 1)
                if n >= 4:
                    pe.wait_ge(rows_low, 16 + n - 3)
                for q in range(4):
                    src = hv[:, 0, t, q * P:(q + 1) * P] if j else nsa[:, t, q * P:(q + 1) * P]
                    ins = nc.tensor.transpose(ps[:, n % 4, q * P:(q + 1) * P], src, eye[:])
                ins.then_inc(rowsT_done, 1)
            pe.wait_ge(rows_low, 32)
            for j in range(16):
                rows_chunk(pe, W_OUT_AT, j, BW, wo_full,
                           (lambda b: pe.wait_ge(res_out, b + 1)) if j >= KC else None)

            pe.wait_ge(res_out, 16)
            for t in range(NT):
                transpose_rows(pe, 2, t, row2)
            pe.wait_ge(rows_low, 48)

            with pe.Fori(0, NF) as i:
                n = i * 16 + MLP_AT
                for j in range(KC):
                    cols_chunk(pe, n, j, m1_full, lambda b: pe.wait_ge(res_out, i * 16 + (8 + b + 1)))
                for j in range(KC):
                    half, fc = divmod(j, 4)
                    s_ = (KC + j) % RING
                    pe.wait_ge(w_split, n + (KC + j + 1))
                    if half == 0:
                        pe.wait_ge(h_low, i * 8 + (2 * fc + 2))
                    for t in range(NT):
                        if fc == 0:
                            if half == 0:
                                pe.wait_ge(m1_out, i * 8 + (t + 1))
                            else:
                                pe.wait_ge(res_out, i * 16 + (16 + t + 1))
                        a = [h[:, fc, t * P:(t + 1) * P] for h in (h1_H, h1_L)]
                        r = [w[:, s_, :] for w in (w_high, w_low)]
                        ins = three_passes(ps[:, t, :], a, r, fc == 0, fc == 3)
                        if t == 7:
                            ins.then_inc(w_used, 1)
                        elif fc == 3:
                            ins.then_inc(m2_full, 1)


_INS = ["x", "attn_norm", "w_in", "q_norm", "k_norm", "cmp_pe_k", "cmp_w1_k", "cmp_w2_k", "cmp_pe_v", "cmp_w1_v",
        "cmp_w2_v", "nsa_out_norm", "hgrn_lb", "hgrn_out_norm", "w_out", "mlp_norm", "w_mlp_in", "w_mlp_out"]


def kernel(**inputs):
    import numpy as _np
    import concourse.bacc as _bacc
    from concourse import mybir as _mybir
    from concourse.bass_utils import run_bass_kernel_spmd as _run

    nc = _bacc.Bacc("TRN2", target_bir_lowering=False, num_devices=1)
    arrays, args = {}, []
    data = {name: _np.ascontiguousarray(inputs[name]) for name in _INS}
    data.update(constants())
    for name, a in data.items():
        arrays[f"in_{name}_dram"] = a
        args.append(nc.dram_tensor(f"in_{name}_dram", a.shape, _mybir.dt.from_np(a.dtype), kind="ExternalInput").ap())
    out = nc.dram_tensor("out_0_dram", (1, S, D), _mybir.dt.float32, kind="ExternalOutput").ap()
    program(nc, *args, out)
    r = _run(nc, [arrays], core_ids=[0])
    return r.results[0]["out_0_dram"]
```
